# Optimizing a Trainium2 kernel written in Bass

```python
import math
import jax, jax.numpy as jnp
from jax import lax
import numpy as np

D_MODEL = 2048
BATCH = 1
SEQ = 256
DEPTH = 2
DEC_BATCH = 8
DEC_SEQ = 4
PAST_LEN = 2048
PAGE_SIZE = 128

N_MIXERS = 2
N_HG = (DEPTH + 1) // 2
N_GLA = DEPTH // 2
HG_KEY = 128
HG_HEADS = D_MODEL // HG_KEY
HG_VAL = D_MODEL // HG_HEADS
HG_DIM = HG_HEADS * HG_KEY
GLA_HEADS = 4
GLA_KEY_DIM = D_MODEL // 2
GLA_VAL_DIM = D_MODEL
GLA_KEY = GLA_KEY_DIM // GLA_HEADS
GLA_VAL = GLA_VAL_DIM // GLA_HEADS
GLA_RANK = 16
GLA_GATE_NORM = 16.0
GLA_IN = 2 * GLA_KEY_DIM + 2 * GLA_VAL_DIM + GLA_RANK
D_FF = 4 * D_MODEL
CHUNK = 64
ALPHA = (2.0 * DEPTH) ** 0.25
BETA = (8.0 * DEPTH) ** -0.25
EPS = 1e-5

kernel_name = "hgrn2_gla_adaln_deepnorm_step"

def layer_norm(x, w, b):
    xf = x.astype(jnp.float32)
    mu = jnp.mean(xf, -1, keepdims=True)
    xc = xf - mu
    var = jnp.mean(xc * xc, -1, keepdims=True)
    return (xc * lax.rsqrt(var + EPS) * w.astype(jnp.float32) + b.astype(jnp.float32)).astype(x.dtype)

def head_rms_norm(o, w):
    of = o.astype(jnp.float32)
    of = of * lax.rsqrt(jnp.mean(of * of, -1, keepdims=True) + EPS)
    return (of * w.astype(jnp.float32)).astype(o.dtype)

def gated_linear_recurrence(q, k, v, log_f, s0):
    B, T, H, K = q.shape
    V = v.shape[-1]
    C = CHUNK if T % CHUNK == 0 else T
    N = T // C
    f32 = jnp.float32

    def to_chunks(a):
        return a.astype(f32).reshape(B, N, C, H, a.shape[-1]).transpose(1, 0, 3, 2, 4)

    qc, kc, vc, gc = to_chunks(q), to_chunks(k), to_chunks(v), to_chunks(log_f)
    causal = jnp.tril(jnp.ones((C, C), bool))[None, None, :, :, None]

    def step(S, inp):
        qb, kb, vb, gb = inp
        b = jnp.cumsum(gb, axis=2)
        diff = b[:, :, :, None, :] - b[:, :, None, :, :]
        decay = jnp.exp(jnp.where(causal, diff, -jnp.inf))
        att = jnp.einsum('bhtk,bhsk,bhtsk->bhts', qb, kb, decay)
        o = (jnp.einsum('bhts,bhsv->bhtv', att, vb)
             + jnp.einsum('bhtk,bhkv->bhtv', qb * jnp.exp(b), S))
        b_last = b[:, :, -1:, :]
        S_new = (jnp.exp(b_last[:, :, 0, :])[..., None] * S
                 + jnp.einsum('bhsk,bhsv->bhkv', kb * jnp.exp(b_last - b), vb))
        return S_new, o

    S, o = lax.scan(step, s0.astype(f32), (qc, kc, vc, gc))
    o = o.transpose(1, 0, 3, 2, 4).reshape(B, T, H, V)
    return o.astype(q.dtype), S.astype(s0.dtype)

def hgrn2_mixer(h, w_in, lb, norm_w, w_out, s0):
    B, T, _ = h.shape
    q, f_pre, i, g = jnp.split(h @ w_in, 4, axis=-1)
    fp = f_pre.astype(jnp.float32)
    log_f = jnp.logaddexp(jnp.log(lb), jnp.log1p(-lb) + jax.nn.log_sigmoid(fp))
    k = (1.0 - lb) * jax.nn.sigmoid(-fp)
    hd = lambda a, d: a.reshape(B, T, HG_HEADS, d)
    o, s = gated_linear_recurrence(hd(jax.nn.silu(q), HG_KEY), hd(k.astype(h.dtype), HG_KEY),
                                   hd(i, HG_VAL), hd(log_f, HG_KEY), s0)
    o = head_rms_norm(o, norm_w.reshape(HG_HEADS, HG_VAL)).reshape(B, T, HG_DIM) * jax.nn.silu(g)
    return o @ w_out, s

def gla_mixer(h, w_in, w_gk2, b_gk, norm_w, w_out, s0):
    B, T, _ = h.shape
    q, k, v, g, gk_low = jnp.split(
        h @ w_in, np.cumsum([GLA_KEY_DIM, GLA_KEY_DIM, GLA_VAL_DIM, GLA_VAL_DIM]).tolist(), axis=-1)
    log_f = jax.nn.log_sigmoid((gk_low @ w_gk2 + b_gk).astype(jnp.float32)) / GLA_GATE_NORM
    hd = lambda a, d: a.reshape(B, T, GLA_HEADS, d)
    o, s = gated_linear_recurrence(hd(q * GLA_KEY ** -0.5, GLA_KEY), hd(k, GLA_KEY),
                                   hd(v, GLA_VAL), hd(log_f, GLA_KEY), s0)
    o = head_rms_norm(o, norm_w.reshape(GLA_HEADS, GLA_VAL)).reshape(B, T, GLA_VAL_DIM) * jax.nn.silu(g)
    return o @ w_out, s

def trunk(x, c, s_hg, s_gla, w_ada, b_ada, ln_w, ln_b, hg_w_in, hg_lb, hg_norm_w, hg_w_out,
          gla_w_in, gla_w_gk2, gla_b_gk, gla_norm_w, gla_w_out, w_up, w_down):
    new_hg, new_gla = [], []
    cs = jax.nn.silu(c)
    for l in range(DEPTH):
        mod = (cs @ w_ada[l] + b_ada[l])[:, None, :]
        sh1, sc1, g1, sh2, sc2, g2 = jnp.split(mod, 6, axis=-1)
        h = x * (1.0 + sc1) + sh1
        j = l // N_MIXERS
        if l % N_MIXERS == 0:
            y, s = hgrn2_mixer(h, hg_w_in[j], hg_lb[j], hg_norm_w[j], hg_w_out[j], s_hg[j])
            new_hg.append(s)
        else:
            y, s = gla_mixer(h, gla_w_in[j], gla_w_gk2[j], gla_b_gk[j], gla_norm_w[j], gla_w_out[j], s_gla[j])
            new_gla.append(s)
        x = layer_norm(ALPHA * x + (1.0 + g1) * y, ln_w[l, 0], ln_b[l, 0])
        h = x * (1.0 + sc2) + sh2
        y = jnp.square(jax.nn.relu(h @ w_up[l])) @ w_down[l]
        x = layer_norm(ALPHA * x + (1.0 + g2) * y, ln_w[l, 1], ln_b[l, 1])
    return x, jnp.stack(new_hg), jnp.stack(new_gla)

def setup_inputs(seed: int = 0) -> dict:
    key = jax.random.key(seed)
    ks = jax.random.split(key, 32)
    nrm = lambda k, shape, s: jax.random.normal(k, shape, jnp.float32) * s
    d_sc = D_MODEL ** -0.5
    hg_w_in = jnp.concatenate([
        nrm(ks[0], (N_HG, D_MODEL, HG_DIM), d_sc),
        nrm(ks[1], (N_HG, D_MODEL, HG_DIM), d_sc),
        nrm(ks[2], (N_HG, D_MODEL, HG_DIM), d_sc * BETA),
        nrm(ks[3], (N_HG, D_MODEL, HG_DIM), d_sc)], -1)
    gla_w_in = jnp.concatenate([
        nrm(ks[4], (N_GLA, D_MODEL, GLA_KEY_DIM), d_sc),
        nrm(ks[5], (N_GLA, D_MODEL, GLA_KEY_DIM), d_sc),
        nrm(ks[6], (N_GLA, D_MODEL, GLA_VAL_DIM), d_sc * BETA),
        nrm(ks[7], (N_GLA, D_MODEL, GLA_VAL_DIM), d_sc),
        nrm(ks[8], (N_GLA, D_MODEL, GLA_RANK), d_sc)], -1)
    return {
        "x_prompt": nrm(ks[9], (BATCH, SEQ, D_MODEL), 1.0),
        "x_sample": nrm(ks[10], (DEC_BATCH, DEC_SEQ, D_MODEL), 1.0),
        "state_hgrn": nrm(ks[11], (N_HG, DEC_BATCH, HG_HEADS, HG_KEY, HG_VAL), 0.5),
        "state_gla": nrm(ks[12], (N_GLA, DEC_BATCH, GLA_HEADS, GLA_KEY, GLA_VAL), 0.5),
        "c_prompt": nrm(ks[13], (BATCH, D_MODEL), 1.0),
        "c_sample": nrm(ks[14], (DEC_BATCH, D_MODEL), 1.0),
        "w_ada": nrm(ks[15], (DEPTH, D_MODEL, 6 * D_MODEL), d_sc * 0.5),
        "b_ada": nrm(ks[16], (DEPTH, 6 * D_MODEL), 0.02),
        "ln_w": 1.0 + nrm(ks[17], (DEPTH, 2, D_MODEL), 0.02),
        "ln_b": nrm(ks[18], (DEPTH, 2, D_MODEL), 0.02),
        "hg_w_in": hg_w_in,
        "hg_lb_raw": nrm(ks[19], (N_HG, HG_DIM), 0.5),
        "hg_norm_w": 1.0 + nrm(ks[20], (N_HG, HG_DIM), 0.02),
        "hg_w_out": nrm(ks[21], (N_HG, HG_DIM, D_MODEL), HG_DIM ** -0.5 * BETA),
        "gla_w_in": gla_w_in,
        "gla_w_gk2": nrm(ks[22], (N_GLA, GLA_RANK, GLA_KEY_DIM), GLA_RANK ** -0.5),
        "gla_b_gk": nrm(ks[23], (N_GLA, GLA_KEY_DIM), 0.1),
        "gla_norm_w": 1.0 + nrm(ks[24], (N_GLA, GLA_VAL_DIM), 0.02),
        "gla_w_out": nrm(ks[25], (N_GLA, GLA_VAL_DIM, D_MODEL), GLA_VAL_DIM ** -0.5 * BETA),
        "w_up": nrm(ks[26], (DEPTH, D_MODEL, D_FF), d_sc),
        "w_down": nrm(ks[27], (DEPTH, D_FF, D_MODEL), D_FF ** -0.5 * BETA),
    }

def reference(x_prompt, x_sample, state_hgrn, state_gla, c_prompt, c_sample, w_ada, b_ada, ln_w, ln_b,
              hg_w_in, hg_lb_raw, hg_norm_w, hg_w_out, gla_w_in, gla_w_gk2, gla_b_gk, gla_norm_w,
              gla_w_out, w_up, w_down):
    p = jax.nn.softmax(hg_lb_raw.astype(jnp.float32), axis=0)
    hg_lb = jnp.clip(jnp.cumsum(p, axis=0) - p[0], 0.0, 1.0 - 1e-6)
    weights = (w_ada, b_ada, ln_w, ln_b, hg_w_in, hg_lb, hg_norm_w, hg_w_out,
               gla_w_in, gla_w_gk2, gla_b_gk, gla_norm_w, gla_w_out, w_up, w_down)
    zero_hg = jnp.zeros((N_HG, x_prompt.shape[0], HG_HEADS, HG_KEY, HG_VAL), state_hgrn.dtype)
    zero_gla = jnp.zeros((N_GLA, x_prompt.shape[0], GLA_HEADS, GLA_KEY, GLA_VAL), state_gla.dtype)
    y_prompt, new_hgrn_prompt, new_gla_prompt = trunk(x_prompt, c_prompt, zero_hg, zero_gla, *weights)
    y_sample, new_hgrn_sample, new_gla_sample = trunk(x_sample, c_sample, state_hgrn, state_gla, *weights)
    return (y_prompt, y_sample, new_hgrn_prompt, new_gla_prompt, new_hgrn_sample, new_gla_sample)


_drawn_inputs = setup_inputs


def setup_inputs(seed=0):
    import zlib

    import numpy as np

    out = dict(_drawn_inputs(seed))
    spreads = {}
    factors = {'hg_norm_w': 8.0, 'gla_norm_w': 8.0}
    for name, (base, spread) in spreads.items():
        noise = np.random.default_rng([zlib.crc32(name.encode()), seed]).standard_normal(out[name].shape)
        drawn = base * np.exp(spread * noise) if base else spread * noise
        out[name] = __import__('jax').numpy.asarray(drawn.astype(out[name].dtype))
    for name, factor in factors.items():
        out[name] = (out[name] * factor).astype(out[name].dtype)
    return out
```

```python
import numpy as np

import concourse.bass as bass
from concourse import mybir

F32 = mybir.dt.float32
F32R = mybir.dt.float32r
U8 = mybir.dt.uint8
ALU = mybir.AluOpType
ACT = mybir.ActivationFunctionType
AX = mybir.AxisListType

P = 128
D = 2048
KB = D // P
TP, NB, TB = 256, 8, 4
TS = NB * TB
T = TP + TS
NSEQ = 1 + NB
DEPTH = 2
FF = 4 * D
ALPHA = (2.0 * DEPTH) ** 0.25
EPS = 1e-5
GLA_HEADS, GLA_K, GLA_V, GLA_RANK = 4, 256, 512, 16
HG_PAIRS = 8
GATE_NORM = 16.0
LB_LEAST = 2.0 ** -60
NLEVEL = 9
RING = 8
SPLIT = 4
AHEAD = 3
ADA_W = 1024


class Stage:

    def __init__(self, before, iters, steps, ada=None, emptied_by=""):
        self.before, self.iters, self.steps = before, iters, steps
        self.emptied_by = emptied_by
        self.emptied0 = {e: before.emptied0[e] + before.iters * before.emptied_by.count(e) if before else 0 for e in "AV"}
        self.ada = ada or {}
        self.n_ada = sum(self.ada.values())
        order = [("w", g) for g in range(min(AHEAD, steps))]
        a = 0
        for s in range(max(steps, 1)):
            for _ in range(self.ada.get(s, 0)):
                order.append(("a", a))
                a += 1
            if s + AHEAD < steps:
                order.append(("w", s + AHEAD))
        self.order = order
        self.place = {item: pos for pos, item in enumerate(order)}
        self.per = len(order)
        self.w0 = before.w0 + before.iters * before.steps if before else 0
        self.p0 = before.p0 + before.iters * len(before.emptied_by) if before else 0
        self.a0 = before.a0 + before.iters * before.n_ada if before else 0
        self.r0 = before.r0 + before.iters * before.per if before else 0
        assert iters == 1 or (self.per % RING == 0 and steps % SPLIT == 0)

    def tile(self, n, g):
        return self.w0 + n * self.steps + g

    def emptied(self, n, p):
        e = self.emptied_by[p]
        return e, self.emptied0[e] + n * self.emptied_by.count(e) + self.emptied_by[:p + 1].count(e)

    def bank(self, p):
        return 2 * ((self.p0 + p) % 2)

    def bank_free(self, n, p):
        if p >= 2:
            return self.emptied(n, p - 2)
        st, p = self, p - 2
        if not isinstance(n, int) or n > 0:
            return self.emptied(n - 1, p + len(self.emptied_by))
        while p < 0:
            st = st.before
            if st is None or not st.emptied_by:
                return None
            p += len(st.emptied_by) * st.iters
        return st.emptied(p // len(st.emptied_by), p % len(st.emptied_by))

    def split_slot(self, g):
        return (self.w0 + g) % SPLIT

    def ring(self, n, kind, i):
        if kind == "w" and i >= self.steps:
            pos = self.per + i - self.steps
        else:
            pos = self.place[(kind, i)]
        if isinstance(n, int):
            r = self.r0 + n * self.per + pos
            return r % RING, r // RING + 1
        return (self.r0 + pos) % RING, (self.r0 + pos) // RING + 1 + n * (self.per // RING)

    def evicted(self, n, pos):
        st, n, pos = self, n, pos - RING
        while pos < 0:
            if isinstance(n, int) and n == 0:
                st = st.before
                if st is None:
                    return None
                n, pos = st.iters - 1, pos + st.per
            else:
                n, pos = n - 1, pos + st.per
        kind, i = st.order[pos]
        return kind, (st.w0 + n * st.steps if kind == "w" else st.a0 + n * st.n_ada) + i


ADA0 = Stage(None, 4, 0, {0: KB})
HG = Stage(ADA0, HG_PAIRS, 16, {3: 3, 4: 3, 5: 3, 6: 3, 7: 4}, "AVAV")
HGO = Stage(HG, 1, 32, emptied_by="V" * 8)
MLP0 = Stage(HGO, 4, 64, {s: 1 for s in range(48)}, "A" * 8 + "V" * 8)
LOW = Stage(MLP0, 1, 4, emptied_by="A")
GLA = Stage(LOW, GLA_HEADS, 24, emptied_by="AAAAVV")
GLO = Stage(GLA, 1, 32, emptied_by="V" * 8)
MLP1 = Stage(GLO, 4, 64, emptied_by="A" * 8 + "V" * 8)
OUT_ORDER = [(0, 0), (0, 1), (0, 2), (1, 0), (1, 1), (1, 2), (0, 3), (1, 3)] + [
    (p, t) for p in range(2, 8) for t in range(4)]
OUT_DONE = [6, 7] + [4 * p + 3 for p in range(2, 8)]


class Memory:

    def __init__(self, nc):
        self.nc = nc
        self.at = (nc.sbuf_base + 31) // 32 * 32
        self.top = nc.sbuf_usable_end

    def put(self, name, shape, dtype=F32, at=None):
        size = int(np.prod(shape[1:])) * (1 if dtype == U8 else 4)
        size = (size + 31) // 32 * 32
        start = self.at if at is None else at
        assert start + size <= self.top, (name, start + size - self.top)
        t = self.nc.alloc_sbuf_tensor_at(name, list(shape), dtype, offset=start)
        if at is None:
            self.at = start + size
        return t

    def scratch(self, regions, items):
        out, spots = {}, [list(r) for r in regions]
        for name, shape, *dtype in items:
            dt = dtype[0] if dtype else F32
            size = (int(np.prod(shape[1:])) * (1 if dt == U8 else 4) + 31) // 32 * 32
            spot = next((s for s in spots if s[0] + size <= s[1]), None)
            assert spot, (name, size, spots)
            out[name.split(".")[1]] = self.put(name.replace(".", "_"), shape, dt, at=spot[0])
            spot[0] += size
        return out


def build_program(nc, A):
    mem = Memory(nc)
    raw = mem.put("raw", [P, RING, 1024])
    w_hi = mem.put("w_hi", [P, SPLIT, 4, 256], F32R)
    w_lo = mem.put("w_lo", [P, SPLIT, 4, 256], F32R)
    a_hi = mem.put("a_hi", [P, KB, T], F32R)
    a_lo = mem.put("a_lo", [P, KB, T], F32R)
    z = mem.put("z", [P, KB, T])
    mod_at = mem.at
    mod = mem.put("mod", [P, DEPTH, 6 * KB, NSEQ])
    ident = mem.put("ident", [P, P])
    ones = mem.put("ones", [P, P])
    masks = mem.put("masks", [P, 8, P], U8)
    bmask = mem.put("bmask", [P, NB])
    b_ada = mem.put("b_ada_t", [P, DEPTH, 6 * KB])
    lnv = mem.put("lnv", [P, 2, DEPTH, 2, KB])
    vec = mem.put("vec", [P, 56])
    lbv = mem.put("lbv", [P, 4, KB])
    eps = mem.put("eps", [P, 1])
    c_t = mem.put("c_t", [P, KB, 32])
    c1_at = mem.at
    c1 = mem.put("c1", [P, KB, NSEQ])
    c0 = mem.put("c0", [P, KB, NSEQ])
    awb = mem.put("awb", [P, 2, KB])
    mu = mem.put("mu", [P, T])
    rstd = mem.put("rstd", [P, T])
    act0 = mem.at
    act_hi = mem.put("act_hi", [P, KB, T], F32R)
    act_lo = mem.put("act_lo", [P, KB, T], F32R)
    half, act1, end = act0 + KB * T * 4, mem.at, mem.top

    o_buf = mem.put("o_buf", [P, KB, T], at=act0)
    boot = mem.scratch([(act0, act1), (act1, end)], [
        ("boot.x", [P, 3, D]), ("boot.c", [P, D]), ("boot.rows", [P, 4, P]), ("boot.masks", [P, 8, P]), ("boot.c_f", [P, KB, NSEQ]),
        ("boot.c_e", [P, KB, NSEQ]), ("boot.ada", [P, 256])])
    ln = mem.scratch([(act0, act1)], [("ln.sq", [P, KB, T]), ("ln.h", [P, 2, 4, T])])
    mlp_b = mem.scratch([(act1, end)], [("mlp.r", [P, 2, 2, T]), ("mlp.ada", [P, 768]), ("mlp.zs", [P, 2, TS])])
    common = lambda m: [(f"{m}.x", [P, 2, 2, T]), (f"{m}.q", [P, 2, T]), (f"{m}.k", [P, 2, T]),
                        (f"{m}.pre", [P, 2, T]), (f"{m}.suf", [P, 2, T]), (f"{m}.qd", [P, 2, TS]),
                        (f"{m}.dec", [P, 2, NB])]
    hg = mem.scratch([(half, act1), (act1, end)], common("hg") + [
        ("hg.v", [P, 2, T]), ("hg.g", [P, 2, T]), ("hg.att", [P, 2, 3, P]), ("hg.atts", [32, 2, TS]),
        ("hg.tm", [P, 2, 4, P]), ("hg.ts", [32, 4, P]), ("hg.vsm", [32, 2, NB, P]), ("hg.sq", [P, T]),
        ("hg.s0", [P, 2, NB, P]), ("hg.sp", [P, 2, P]), ("hg.ada", [P, 256])])
    gl = mem.scratch([(mod_at, mod_at + 6 * KB * NSEQ * 4), (c1_at, c1_at + 2 * KB * NSEQ * 4),
                      (half, act1), (act1, end)],
                     [("gl.sp", [P, GLA_V]), ("gl.low", [P, T])] + common("gl") + [
        ("gl.v", [P, 4, T]), ("gl.g", [P, 4, T]), ("gl.att", [P, 3, P]), ("gl.atts", [32, TS]),
        ("gl.vt", [P, 2, GLA_V]), ("gl.kt", [P, 2, 2, P]), ("gl.vs", [32, GLA_V]), ("gl.ks", [32, 2, P]),
        ("gl.ksm", [32, 2, 2, P]), ("gl.s0", [P, 4, 2, GLA_V]), ("gl.gk2", [P, 2, P])])
    yout = mem.scratch([(act0, act1)], [("yout.y", [P, 3, D])])["y"]

    main = nc.alloc_psum_tensor("main", [P, 4, 512], F32)
    b4, b5, b6, b7 = (nc.alloc_psum_tensor(f"bank{i}", [P, 512], F32) for i in (4, 5, 6, 7))

    sems = {}

    def S(name):
        if name not in sems:
            sems[name] = nc.alloc_semaphore(name)
        return sems[name]

    raw_loaded = [S(f"raw_loaded{i}") for i in range(RING)]
    hi_ready = S("hi_ready")
    lo_ready = S("lo_ready")
    tile_done = S("tile_done")
    ada_used = S("ada_used")
    panel_read = {"A": S("panel_read_act"), "V": S("panel_read_dve")}
    act_step, dve_step, pool_step = S("act_step"), S("dve_step"), S("pool_step")
    ada_copied = S("ada_copied")
    ada_turned = S("ada_turned")
    mod_ready = S("mod_ready")
    boot_loaded, boot_set = S("boot_loaded"), S("boot_set")
    boot_turned, boot_read = S("boot_turned"), S("boot_read")
    c_exp, c_ready, lb_exp, lb_ready, lb_logs = S("c_exp"), S("c_ready"), S("lb_exp"), S("lb_ready"), S("lb_logs")
    a_float = S("a_float")
    a_sample = S("a_sample")
    a_high = S("a_high")
    a_ready = S("a_ready")
    act_high, act_ready = S("act_high"), S("act_ready")
    ln_sum, ln_mean, ln_centered = S("ln_sum"), S("ln_mean"), S("ln_centered")
    ln_squared, ln_var, ln_rstd, ln_scaled = S("ln_squared"), S("ln_var"), S("ln_rstd"), S("ln_scaled")
    y_turned, y_read, y_stored = S("y_turned"), S("y_read"), S("y_stored")
    y_ready = S("y_ready")
    h_terms = S("h_terms")
    act_base = {2: 0, 5: 8 * MLP0.iters}

    def mixer(m, slots):
        names = ("gate_log gate_lin gate_mix gate_soft gates_ready k_ready silu_exp exp_ready sums_ready "
                 "level_ready level_done level_read kd_exp kd_ready turned turned_read s_turned "
                 "s_turned_read s_masked o_done o_read oi_done oi_read squared summed rstd_ready o_ready "
                 "att_set ps_done ps_read ps_stored ss_done ss_read gk_done gk_read gk2_loaded gk2_set").split()
        return {name: S(f"{m}_{name}") for name in names} | {
            name: [S(f"{m}_{name}{i}") for i in range(slots)] for name in ("s0_loaded", "s0_stored")}

    H, G = mixer("hg", 2), mixer("gl", 4)

    w_ada, w_up, w_down = A["w_ada"], A["w_up"], A["w_down"]
    hg_in, hg_out, gla_in, gla_out = A["hg_w_in"][0], A["hg_w_out"][0], A["gla_w_in"][0], A["gla_w_out"][0]

    def cols(start, size=256):
        return slice(start, start + size) if isinstance(start, int) else bass.ds(start, size)

    def weights(w, row, col):
        return w[cols(row, 512), :].rearrange("(k p) n -> p k n", p=P)[:, :, cols(col)]

    def halves(t, L, second):
        m = 1 << (L - 1)
        if L <= 2:
            v = t.rearrange("p h t -> p (h t)").rearrange("p (b c) -> p b c", c=2 * m)
            return v[:, :, m:] if second else v[:, :, :m]
        v = t[:, :, 0:TP].rearrange("p h (b c) -> p h b c", c=2 * m)
        return v[:, :, :, m:] if second else v[:, :, :, :m]

    def last_of(v):
        m = v.shape[-1]
        v = v[:, :, m - 1:m] if len(v.shape) == 3 else v[:, :, :, m - 1:m]
        return v.to_broadcast([*v.shape[:-1], m])

    def sample_last(t):
        return t[:, :, TP:T].rearrange("p h (b t) -> p h b t", t=TB)[:, :, :, TB - 1]

    def level_mask(L, n, size=P):
        return masks[0:size, L, 0:size].unsqueeze(1).to_broadcast([size, n, size])

    def seqs(v):
        return v.rearrange("p k (b t) -> p k b t", t=TB)

    def per_token(v):
        return v.unsqueeze(3).to_broadcast([P, v.shape[1], NB, TB])

    def per_seq(v):
        return v.unsqueeze(2).to_broadcast([P, v.shape[1], NSEQ])

    def panel(st, p, n=2):
        return main[:, st.bank(p):st.bank(p) + n, 0:T]

    LAYER_MOD = [(0, 0, 0), (0, 3, 1), (1, 0, 1), (1, 3, 1)]
    hg_state = A["state_hgrn"][0].rearrange("b h k v -> h k b v")
    hg_state_out = A["new_hgrn_sample"][0].rearrange("b h k v -> h k b v")
    gl_state = A["state_gla"][0].rearrange("b h (j k) v -> h b k j v", j=2)
    gl_state_out = A["new_gla_sample"][0].rearrange("b h (j k) v -> h b k j v", j=2)

    def in_register(engine, *values):
        for value in values:
            if not isinstance(value, int):
                engine.compute_val(value)

    block = nc.Block()
    block.__enter__()

    @block.sync
    def _(sp):
        rows = boot["rows"]
        boots = [
            (ident[:, :], A["const_ident"]), (boot["masks"][:, :, :], A["const_masks"]), (bmask[:, :], A["const_bmask"]),
            (rows[0:96, 0, :], A["b_ada"][0].rearrange("(r c) -> r c", c=P)),
            (rows[0:96, 1, :], A["b_ada"][1].rearrange("(r c) -> r c", c=P)),
            (rows[0:64, 2, :], A["ln_w"].rearrange("l i (r c) -> (l i r) c", c=P)),
            (rows[64:128, 2, :], A["ln_b"].rearrange("l i (r c) -> (l i r) c", c=P)),
            (rows[0:16, 3, :], A["hg_lb_raw"][0].rearrange("(r c) -> r c", c=P)),
            (rows[16:32, 3, :], A["hg_norm_w"][0].rearrange("(r c) -> r c", c=P)),
            (rows[32:48, 3, :], A["gla_norm_w"][0].rearrange("(r c) -> r c", c=P)),
            (rows[48:56, 3, :], A["gla_b_gk"][0].rearrange("(r c) -> r c", c=P)),
            (boot["c"][0:1, :], A["c_prompt"]), (boot["c"][1:NSEQ, :], A["c_sample"]),
            (boot["x"][:, 0, :], A["x_prompt"][0, 0:P, :]), (boot["x"][:, 1, :], A["x_prompt"][0, P:TP, :]),
            (boot["x"][0:TS, 2, :], A["x_sample"].rearrange("b t d -> (b t) d")),
        ]
        assert len(boots) == BOOT_LOADS
        for dst, src in boots:
            sp.dma_start(dst, src).then_inc(boot_loaded, 16)

        def load(st, n, source):
            for pos, (kind, i) in enumerate(st.order):
                slot, _ = st.ring(n, kind, i)
                before = st.evicted(n, pos)
                if before:
                    in_register(sp, before[1] + 1)
                    if not isinstance(n, int):
                        sp.wait_ge(boot_loaded, 16)
                    sp.wait_ge(lo_ready if before[0] == "w" else ada_used, before[1] + 1)
                dst = raw[:, slot, :]
                if kind == "w":
                    dst = dst.rearrange("p (k n) -> p k n", k=4)
                sp.dma_start(dst, source(n, kind, i)).then_inc(raw_loaded[slot], 16)

        def run(st, source):
            load(st, 0, source)
            if st.iters > 1:
                with sp.Fori(1, st.iters) as n:
                    load(st, n, source)

        def ada_tile(layer, kb, col):
            return w_ada[layer, kb * P:(kb + 1) * P, cols(col, ADA_W)]

        def hg_tile(n, kind, i):
            if kind == "a":
                return ada_tile(0, i, n * ADA_W + 2 * D)
            return weights(hg_in, i % 4 * 512, n * 256 + (D, 0, 2 * D, 3 * D)[i // 4])

        def mlp_tile(layer):
            def source(n, kind, i):
                if kind == "a":
                    return ada_tile(1, i // 3, n * 3 * ADA_W + i % 3 * ADA_W)
                if i < 32:
                    return weights(w_up[layer], i % 4 * 512, n * D + i // 4 * 256)
                return weights(w_down[layer], n * D + i % 4 * 512, (i // 4 - 8) * 256)
            return source

        def gla_tile(n, kind, i):
            start = (n * 256, n * 256 + GLA_HEADS * GLA_K, n * 512 + D, n * 512 + D + 256,
                     n * 512 + 2 * D, n * 512 + 2 * D + 256)[i // 4]
            return weights(gla_in, i % 4 * 512, start)

        def out_tile(w):
            return lambda n, kind, i: weights(w, OUT_ORDER[i][1] * 512, OUT_ORDER[i][0] * 256)

        run(ADA0, lambda n, kind, i: ada_tile(0, i, n * ADA_W))
        run(HG, hg_tile)
        run(HGO, out_tile(hg_out))
        run(MLP0, mlp_tile(0))
        run(LOW, lambda n, kind, i: weights(gla_in, i * 512, gla_in.shape[1] - 256))
        run(GLA, gla_tile)
        run(GLO, out_tile(gla_out))
        run(MLP1, mlp_tile(1))
        for s in H["s0_stored"]:
            sp.wait_ge(s, 16 * HG_PAIRS)
        for s in G["s0_stored"]:
            sp.wait_ge(s, 16 * GLA_HEADS * 2)
        sp.wait_ge(H["ps_stored"], 16 * HG_PAIRS)
        sp.wait_ge(G["ps_stored"], 16 * GLA_HEADS * 2)
        sp.wait_ge(y_stored, 48)

    @block.tensor
    def _(pe):
        mm, turn = nc.tensor.matmul, nc.tensor.transpose

        def gemm(st, n, g, p, t, x_hi, x_lo, blocks=(0, 1)):
            if t == 0:
                free = st.bank_free(n, p)
                if free:
                    pe.wait_ge(panel_read[free[0]], free[1])
            pe.wait_ge(lo_ready, st.tile(n, g) + 1)
            slot = st.split_slot(g)
            for k in range(4):
                kb = 4 * t + k
                for j in blocks:
                    out = main[:, st.bank(p) + j, 0:T]
                    hi, lo = (w[:, slot, k, j * P:(j + 1) * P] for w in (w_hi, w_lo))
                    mm(out, hi, x_hi[:, kb, :], start=kb == 0, stop=False)
                    mm(out, hi, x_lo[:, kb, :], start=False, stop=False)
                    last = mm(out, lo, x_hi[:, kb, :], start=False, stop=kb == KB - 1)
            last.then_inc(tile_done, 1)

        def ada(st, n, i, kb, bank, col, first):
            slot, count = st.ring(n, "a", i)
            pe.wait_ge(raw_loaded[slot], 16 * count)
            for j in range(4):
                last = mm(bank[32 * j:32 * j + 32, col:col + 256], c_t[:, kb, :], raw[:, slot, j * 256:(j + 1) * 256],
                          start=first, stop=kb == KB - 1, skip_group_check=True, tile_position=(0, 32 * j))
            last.then_inc(ada_used, 1)

        def ada_turn(count, places, src):
            pe.wait_ge(ada_copied, count)
            for i, place in enumerate(places):
                last = turn(place, src[:, i * P:(i + 1) * P], ident[:, :])
            last.then_inc(ada_turned, 1)

        pe.wait_ge(boot_loaded, 16 * BOOT_LOADS)
        pe.wait_ge(boot_set, 1)
        groups = 0

        def turn_group(parts):
            nonlocal groups
            if groups >= 4:
                pe.wait_ge(boot_read, groups - 3)
            for at, src, r in parts:
                last = turn(main[:, groups % 4, at:at + r], src, ident[0:r, 0:r])
            last.then_inc(boot_turned, 1)
            groups += 1

        rows = boot["rows"]
        turn_group([(0, rows[0:96, 0, :], 96), (96, rows[0:96, 1, :], 96)])
        turn_group([(0, rows[:, 2, :], P), (P, rows[0:56, 3, :], 56)])
        turn_group([(NSEQ * kb, boot["c"][0:NSEQ, kb * P:(kb + 1) * P], NSEQ) for kb in range(KB)])
        for i in range(3):
            r = P if i < 2 else TS
            for c in range(4):
                turn_group([(r * j, boot["x"][0:r, i, (4 * c + j) * P:(4 * c + j + 1) * P], r) for j in range(4)])
        pe.wait_ge(c_ready, 1)
        for n in range(4):
            if n:
                pe.wait_ge(ada_copied, n)
            for i in range(KB):
                ada(ADA0, n, i, i, b5, 0, i == 0)
            if n:
                pe.wait_ge(mod_ready, n)
            ada_turn(n + 1, [b7[:, 0:P], b7[:, P:2 * P]], boot["ada"])

        def hg_level(n, L, prev):
            x = hg["x"][:, L % 2]
            lhs, rhs = (hg["k"], hg["q"]) if L == 0 else (x, x)
            bank = b4 if L % 2 == 0 else b5
            if L == 0:
                pe.wait_ge(panel_read["V"], HG.emptied(n, 1)[1])
                pe.wait_ge(H["k_ready"], n + 1)
                if prev:
                    pe.wait_ge(H["ss_read"], 4 * n - 3)
                    pe.wait_ge(H["rstd_ready"], 2 * n)
            else:
                pe.wait_ge(H["level_ready"], 8 * n + L)
            if L == 1:
                pe.wait_ge(ada_copied, 5 + n)
            if L >= 1:
                pe.wait_ge(H["level_read"], 9 * n + (L if L <= 2 else L - 1))
            if L <= 2:
                for h in range(2):
                    mm(b6[0:32, 64 * L + 32 * h:64 * L + 32 * h + 32], lhs[:, h, TP:T], rhs[:, h, TP:T],
                       start=True, stop=True)
            for h in range(2):
                if L == 8:
                    last = mm(bank[:, h * P:(h + 1) * P], x[:, h, 0:P], x[:, h, P:TP], start=True, stop=True)
                else:
                    for t in range(2):
                        c = slice(t * P, (t + 1) * P)
                        last = mm(bank[:, (2 * h + t) * P:(2 * h + t + 1) * P], lhs[:, h, c], rhs[:, h, c],
                                  start=True, stop=True)
            last.then_inc(H["level_done"], 1)

        def hg_turn(pn, h):
            if h == 0:
                pe.wait_ge(H["kd_ready"], pn + 1)
                pe.wait_ge(panel_read["A"], HG.emptied(pn, 2)[1])
                pe.wait_ge(H["level_read"], 9 * pn + 3)
            else:
                pe.wait_ge(H["turned_read"], 2 * pn + 1)
            for j, (src, t) in enumerate([("v", 0), ("v", 1), ("k", 0), ("k", 1)]):
                src = hg["v"] if src == "v" else hg["x"][:, 1]
                last = turn(b6[:, j * P:(j + 1) * P], src[:, h, t * P:(t + 1) * P], ident[:, :])
            last.then_inc(H["turned"], 1)

        def hg_sample_turn(pn):
            pe.wait_ge(mod_ready, 5 + pn)
            for j, (src, h) in enumerate([("v", 0), ("v", 1), ("k", 0), ("k", 1)]):
                src = hg["v"] if src == "v" else hg["x"][:, 1]
                last = turn(b7[0:32, j * P:(j + 1) * P], src[:, h, TP:T], ident[:, :])
            last.then_inc(H["s_turned"], 1)

        def hg_out_head(pn, h):
            pe.wait_ge(H["turned_read"], 2 * pn + h + 1)
            pe.wait_ge(H["s_turned_read"], pn + 1)
            pe.wait_ge(H["level_read"], 9 * pn + 9)
            pe.wait_ge(H["s0_loaded"][h], 16 * (pn + 1))
            if h == 1:
                pe.wait_ge(H["o_read"], 2 * pn + 1)
            tm, att, s0, qd = hg["tm"], hg["att"], hg["s0"], hg["qd"]
            mm(b7[:, 0:TP], tm[:, h, 0, :], att[:, h, 0:2, :].rearrange("p a t -> p (a t)"), start=True, stop=False,
               skip_group_check=True)
            mm(b7[:, P:TP], tm[:, h, 1, :], att[:, h, 2, :], start=False, stop=False, skip_group_check=True)
            mm(b7[:, TP:T], hg["ts"][:, h, :], hg["atts"][:, h, :], start=False, stop=False, skip_group_check=True)
            for b in range(NB):
                last = mm(b7[:, TP + TB * b:TP + TB * (b + 1)], s0[:, h, b, :], qd[:, h, TB * b:TB * (b + 1)],
                          start=False, stop=b == NB - 1, skip_group_check=True)
            last.then_inc(H["o_done"], 1)

        def hg_sum(pn, h):
            pe.wait_ge(H["o_read"], 2 * pn + h + 1)
            if h == 0:
                pe.wait_ge(H["turned_read"], 2 * pn + 2)
            else:
                pe.wait_ge(H["rstd_ready"], 2 * pn + 1)
            mm(b6[:, 0:T], ones[:, :], hg["sq"][:, :], start=True, stop=True).then_inc(H["summed"], 1)

        def hg_prompt_state(pn):
            pe.wait_ge(H["turned_read"], 2 * pn + 2)
            for h in range(2):
                for t in range(2):
                    last = mm(b4[:, h * P:(h + 1) * P], hg["tm"][:, h, 2 + t, :], hg["tm"][:, h, t, :],
                              start=t == 0, stop=t == 1)
            last.then_inc(H["ps_done"], 1)

        def hg_sample_state(pn, x, ada_count):
            h, half_ = divmod(x, 2)
            pe.wait_ge(H["s_masked"], 2 * pn + h + 1)
            if x == 0:
                pe.wait_ge(H["ps_read"], pn + 1)
            elif x == 1:
                pe.wait_ge(H["o_read"], 2 * pn + 2)
            elif x == 2:
                pe.wait_ge(ada_copied, ada_count)
            else:
                pe.wait_ge(H["ss_read"], 4 * pn + 2)
            mm((b4, b7, b5, b7)[x][:, :], hg["ts"][:, 2 + h, :],
               hg["vsm"][:, h, 4 * half_:4 * half_ + 4, :].rearrange("p b v -> p (b v)"), start=True, stop=True
               ).then_inc(H["ss_done"], 1)

        def hg_step(n, s, own, prev):
            pn = n - 1
            if prev:
                if s == 0:
                    hg_level(pn, 6, False)
                elif s == 1:
                    hg_level(pn, 7, False)
                elif s == 2:
                    hg_level(pn, 8, False)
                elif s == 3:
                    hg_turn(pn, 0)
                    hg_sample_turn(pn)
                elif s == 4:
                    hg_turn(pn, 1)
                elif s == 5:
                    hg_out_head(pn, 0)
                elif s == 6:
                    hg_sum(pn, 0)
                    hg_prompt_state(pn)
                elif s == 7:
                    hg_out_head(pn, 1)
                elif s == 8:
                    hg_sum(pn, 1)
                    hg_sample_state(pn, 0, None)
                elif s == 9:
                    hg_sample_state(pn, 1, None)
                    hg_sample_state(pn, 2, 5 + n if own else 4 + n)
                elif s == 10:
                    hg_sample_state(pn, 3, None)
            if own:
                if s in HG.ada:
                    first = sum(c for t, c in HG.ada.items() if t < s)
                    if first == 0 and prev:
                        pe.wait_ge(H["level_read"], 9 * n - 1)
                    for i in range(first, first + HG.ada[s]):
                        ada(HG, n, i, i, b5, 0, i == 0)
                if s >= 10:
                    hg_level(n, s - 10, prev)
                if s == 12:
                    if prev:
                        pe.wait_ge(H["ss_read"], 4 * n)
                    ada_turn(5 + n, [b7[:, 0:P], b7[:, P:2 * P]], hg["ada"])

        def hg_iteration(n, prev):
            for s in range(16):
                hg_step(n, s, True, prev)
                if s < 4 and isinstance(n, int):
                    pe.wait_ge(a_ready, s + 1)
                gemm(HG, n, s, s // 4, s % 4, a_hi, a_lo)

        def out_projection(st, tail, event):
            for s, (p, t) in enumerate(OUT_ORDER):
                for x in ((2 * s, 2 * s + 1) if s < 5 else (10, 11, 12) if s == 5 else ()):
                    tail(x)
                if s < 3 or s == 6:
                    pe.wait_ge(a_ready, 4 * event + t + 1)
                gemm(st, 0, s, p, t, a_hi, a_lo)

        def layer_norm(i, event):
            pe.wait_ge(ln_sum, i + 1)
            mm(b4[:, 0:T], ones[:, :], mu[:, :], start=True, stop=True).then_inc(ln_mean, 1)
            for c in range(4):
                pe.wait_ge(ln_squared, 4 * i + c + 1)
                for kb in range(4 * c, 4 * c + 4):
                    last = mm(b5[:, 0:T], ones[:, :], ln["sq"][:, kb, :], start=kb == 0, stop=kb == KB - 1)
            last.then_inc(ln_var, 1)

        def mlp(st, event, with_ada):
            with pe.Fori(0, st.iters) as n:
                for s in range(64):
                    if s < 4:
                        pe.wait_ge(a_ready, 4 * event + s + 1)
                    if 32 <= s < 36:
                        for kp in (1, 2):
                            pe.wait_ge(act_ready, act_base[event] + 8 * n + 2 * (s - 32) + kp)
                    up = s < 32
                    gemm(st, n, s, s // 4, s % 4, *((a_hi, a_lo) if up else (act_hi, act_lo)))
                    if with_ada and s in st.ada:
                        kb, c = divmod(s, 3)
                        if s == 0:
                            pe.wait_ge(mod_ready, 12 + n)
                        ada(st, n, s, kb, (b4, b4, b5)[c], (0, 256, 0)[c], kb == 0 and c != 1)
                    if with_ada and s == 52:
                        ada_turn(13 + n, [b6[:, i * P:(i + 1) * P] for i in range(4)] +
                                 [b7[:, i * P:(i + 1) * P] for i in range(2)], mlp_b["ada"])

        hg_iteration(0, False)
        with pe.Fori(1, HG_PAIRS) as n:
            hg_iteration(n, True)
        out_projection(HGO, lambda s: hg_step(HG_PAIRS, s, False, True), 1)
        layer_norm(0, 2)
        mlp(MLP0, 2, True)
        layer_norm(1, 3)

        def gl_level(n, L, prev):
            x = gl["x"][:, L % 2]
            lhs, rhs = (gl["k"], gl["q"]) if L == 0 else (x, x)
            bank = b4 if L % 2 == 0 else b5
            if L == 0:
                pe.wait_ge(panel_read["A"], GLA.emptied(n, 1)[1])
                if prev:
                    pe.wait_ge(G["ss_read"], 8 * n)
                    pe.wait_ge(G["o_read"], 4 * n)
            else:
                pe.wait_ge(G["level_ready"], 8 * n + L)
            if L == 1 and prev:
                pe.wait_ge(G["rstd_ready"], n)
            if L >= 1:
                pe.wait_ge(G["level_read"], 9 * n + (L if L <= 2 else L - 1))
            if L <= 2:
                for j in range(2):
                    mm(b6[0:32, 32 * L:32 * L + 32], lhs[:, j, TP:T], rhs[:, j, TP:T], start=j == 0, stop=j == 1)
            tiles = [(slice(0, P), slice(P, TP))] if L == 8 else [(slice(t * P, (t + 1) * P),) * 2 for t in range(2)]
            for t, (rows_, cols_) in enumerate(tiles):
                for j in range(2):
                    last = mm(bank[:, t * P:(t + 1) * P], lhs[:, j, rows_], rhs[:, j, cols_], start=j == 0, stop=j == 1)
            last.then_inc(G["level_done"], 1)

        def gl_gate(n, j, prev):
            if j == 0:
                if prev:
                    pe.wait_ge(G["ps_read"], 2 * n)
                else:
                    pe.wait_ge(panel_read["A"], LOW.emptied(0, 0)[1])
                pe.wait_ge(G["gk2_loaded"], 16 * (n + 1))
            else:
                pe.wait_ge(G["gk_read"], 2 * n + 1)
            mm(b6[:, 0:T], gl["gk2"][:, j, :], gl["low"][:, :],
               start=True, stop=True).then_inc(G["gk_done"], 1)

        def gl_turn_v(n, t):
            if t == 0:
                pe.wait_ge(panel_read["A"], GLA.emptied(n, 3)[1])
                pe.wait_ge(G["level_read"], 9 * n + 3)
            bank = (b6, b7)[t]
            for j in range(4):
                last = turn(bank[:, j * P:(j + 1) * P], gl["v"][:, j, t * P:(t + 1) * P], ident[:, :])
            last.then_inc(G["turned"], 1)

        def gl_turn_vs(n):
            pe.wait_ge(G["turned_read"], 3 * n + 1)
            for j in range(4):
                last = turn(b6[0:32, j * P:(j + 1) * P], gl["v"][:, j, TP:T], ident[:, :])
            last.then_inc(G["s_turned"], 1)

        def gl_turn_k(n):
            pe.wait_ge(G["kd_ready"], n + 1)
            pe.wait_ge(G["level_read"], 9 * n + 8)
            for t in range(2):
                for j in range(2):
                    last = turn(b5[:, (2 * t + j) * P:(2 * t + j + 1) * P], gl["x"][:, 1, j, t * P:(t + 1) * P],
                                ident[:, :])
            last.then_inc(G["turned"], 1)
            pe.wait_ge(G["turned_read"], 3 * n + 2)
            for j in range(2):
                last = turn(b7[0:32, j * P:(j + 1) * P], gl["x"][:, 1, j, TP:T], ident[:, :])
            last.then_inc(G["s_turned"], 1)

        def gl_prompt_state(n, j):
            if j == 0:
                pe.wait_ge(G["turned_read"], 3 * n + 3)
                pe.wait_ge(G["s_turned_read"], 2 * n + 1)
            else:
                pe.wait_ge(G["ps_read"], 2 * n + 1)
            for t in range(2):
                last = mm(b6[:, :], gl["kt"][:, t, j, :], gl["vt"][:, t, :], start=t == 0, stop=t == 1)
            last.then_inc(G["ps_done"], 1)

        def gl_intra(n):
            pe.wait_ge(G["s_turned_read"], 2 * n + 2)
            pe.wait_ge(G["level_read"], 9 * n + 3)
            for v in range(4):
                mm(b7[:, 32 * v:32 * v + 32], gl["vs"][:, v * P:(v + 1) * P], gl["atts"][:, :], start=v == 0,
                   stop=False, skip_group_check=True)

        def gl_sample(n, b):
            slot = b % 4
            pe.wait_ge(G["s0_loaded"][slot], 32 * n + 16 * (b // 4 + 1))
            pe.wait_ge(G["s_masked"], 8 * n + b + 1)
            if b == 0:
                pe.wait_ge(G["level_read"], 9 * n + 9)
                pe.wait_ge(G["turned_read"], 3 * n + 3)
            else:
                pe.wait_ge(G["ss_read"], 8 * n + b)
            for v in range(4):
                for j in range(2):
                    last = mm(b7[:, 32 * v + TB * b:32 * v + TB * (b + 1)], gl["s0"][:, slot, j, v * P:(v + 1) * P],
                              gl["qd"][:, j, TB * b:TB * (b + 1)], start=False, stop=j == 1 and b == NB - 1,
                              skip_group_check=True)
            if b == NB - 1:
                last.then_inc(G["oi_done"], 1)
            for j, bank in enumerate((b4, b5)):
                last = mm(bank[:, :], gl["ksm"][:, b % 2, j, :], gl["vs"][:, :], start=True, stop=True)
            last.then_inc(G["ss_done"], 1)

        def gl_out_block(n, v):
            bank = (b6, b7)[v % 2]
            if v == 1:
                pe.wait_ge(G["oi_read"], n + 1)
            if v >= 2:
                pe.wait_ge(G["o_read"], 4 * n + v - 1)
            mm(bank[:, 0:TP], gl["vt"][:, 0, v * P:(v + 1) * P], gl["att"][:, 0:2, :].rearrange("p a t -> p (a t)"),
               start=True, stop=False, skip_group_check=True)
            mm(bank[:, P:TP], gl["vt"][:, 1, v * P:(v + 1) * P], gl["att"][:, 2, :], start=False, stop=True,
               skip_group_check=True).then_inc(G["o_done"], 1)

        def gl_sum(n):
            pe.wait_ge(G["squared"], n + 1)
            pe.wait_ge(G["ss_read"], 8 * n + 8)
            for v in range(4):
                last = mm(b5[:, 0:T], ones[:, :], gl["v"][:, v, :], start=v == 0, stop=v == 3)
            last.then_inc(G["summed"], 1)

        def gl_step(n, s, own, prev):
            pn = n - 1
            if prev:
                if s <= 6:
                    gl_sample(pn, s + 1)
                if s == 0:
                    gl_prompt_state(pn, 1)
                if s in (6, 8):
                    if s == 6:
                        pe.wait_ge(*((G["gk_read"], 2 * n + 2) if own else (G["ps_read"], 2 * pn + 2)))
                    gl_out_block(pn, 0 if s == 6 else 1)
                if s == 8:
                    gl_out_block(pn, 2)
                if s == 9:
                    gl_out_block(pn, 3)
                if s == 11:
                    gl_sum(pn)
            if own:
                if s == 2:
                    gl_gate(n, 0, prev)
                elif s == 4:
                    gl_gate(n, 1, prev)
                elif 11 <= s <= 19:
                    gl_level(n, s - 11, prev)
                if s == 17:
                    gl_turn_v(n, 0)
                    gl_turn_v(n, 1)
                elif s == 19:
                    gl_turn_vs(n)
                elif s == 20:
                    gl_turn_k(n)
                elif s == 22:
                    gl_prompt_state(n, 0)
                elif s == 23:
                    gl_intra(n)
                    gl_sample(n, 0)

        for s in range(4):
            pe.wait_ge(a_ready, 4 * 3 + s + 1)
            gemm(LOW, 0, s, 0, s, a_hi, a_lo, blocks=(1,))

        def gl_iteration(n, prev):
            for s in range(24):
                gl_step(n, s, True, prev)
                gemm(GLA, n, s, s // 4, s % 4, a_hi, a_lo)

        gl_iteration(0, False)
        with pe.Fori(1, GLA_HEADS) as n:
            gl_iteration(n, True)
        out_projection(GLO, lambda s: gl_step(GLA_HEADS, s, False, True), 4)
        layer_norm(2, 5)
        mlp(MLP1, 5, False)
        layer_norm(3, None)

        for i in range(3):
            r = P if i < 2 else TS
            for c in range(4):
                g = 4 * i + c
                pe.wait_ge(y_ready, c + 1)
                if g >= 4:
                    pe.wait_ge(y_read, g - 3)
                for j in range(4):
                    last = turn(main[0:r, g % 4, j * P:(j + 1) * P], z[:, 4 * c + j, i * P:i * P + r], ident[:, :])
                last.then_inc(y_turned, 1)

    @block.scalar
    def _(act):
        tally = Tally(act, act_step)
        step = tally.step
        F = nc.scalar.activation

        def cast(st, n, g):
            slot, count = st.ring(n, "w", g)
            act.wait_ge(raw_loaded[slot], 16 * count)
            if not isinstance(n, int) or st.tile(n, g) >= SPLIT:
                act.wait_ge(tile_done, st.tile(n, g) - (SPLIT - 1))
            F(w_hi[:, st.split_slot(g)].rearrange("p k n -> p (k n)"), raw[:, slot, :], ACT.Copy).then_inc(hi_ready, 1)

        def panel_done(st, n, g):
            act.wait_ge(tile_done, st.tile(n, g) + 1)

        def split_h(e, first, src_sem=None, src_base=0):
            for c in range(4):
                if src_sem is not None:
                    act.wait_ge(src_sem, src_base + c + 1)
                if c >= 2:
                    act.wait_ge(a_ready, 4 * e + c - 1)
                for i in range(4):
                    kb = 4 * c + i
                    last = F(ln["h"][:, c % 2, i, 0:TP], z[:, kb, 0:TP], ACT.Identity, scale=c1[:, kb, 0:1],
                             bias=c0[:, kb, 0:1])
                last.then_inc(a_float, 1)
                act.wait_ge(a_float, 4 * first + c + 1)
                act.wait_ge(a_sample, 4 * first + c + 1)
                F(a_hi[:, 4 * c:4 * c + 4, :], ln["h"][:, c % 2], ACT.Copy).then_inc(a_high, 1)

        def split_o(c):
            F(a_hi[:, 4 * c:4 * c + 4, :], o_buf[:, 4 * c:4 * c + 4, :], ACT.Copy).then_inc(a_high, 1)

        act.wait_ge(boot_set, 1)
        act.wait_ge(boot_read, 3)
        F(boot["c_e"][:, :, :], boot["c_f"][:, :, :], ACT.Exp, scale=-1.0).then_inc(c_exp, 1)
        act.wait_ge(lb_ready, 1)
        F(lbv[:, 0, :], lbv[:, 0, :], ACT.Exp).then_inc(lb_exp, 1)
        act.wait_ge(lb_ready, 2)
        F(lbv[:, 1, :], lbv[:, 0, :], ACT.Ln, scale=-1.0, bias=ones[:, 0:1])
        F(lbv[:, 2, :], lbv[:, 3, :], ACT.Ln).then_inc(lb_logs, 1)
        for n in range(4):
            act.wait_ge(ada_used, KB * (n + 1))
            if n:
                act.wait_ge(ada_turned, n)
            F(boot["ada"][:, :], b5[:, 0:256], ACT.Copy).then_inc(ada_copied, 1)
        act.wait_ge(boot_turned, 15)
        for g in range(AHEAD):
            cast(HG, 0, g)
        act.wait_ge(h_terms, 1)
        split_h(0, 0)

        def silu_exp(M, dst, src):
            F(dst, src, ACT.Exp, scale=-1.0).then_inc(M["silu_exp"], 1)

        def level_exp(M, buf, n, L):
            if L == 1:
                act.wait_ge(M["gates_ready"], n + 1)
            else:
                act.wait_ge(M["sums_ready"], 8 * n + L - 1)
            if L >= 3:
                act.wait_ge(M["level_done"], 9 * n + L - 1)
            x = buf["x"][:, L % 2]
            F(halves(x, L, False), halves(buf["suf"], L, False), ACT.Exp)
            F(halves(x, L, True), halves(buf["pre"], L, True), ACT.Exp).then_inc(M["exp_ready"], 1)

        def key_exp(M, buf, n):
            act.wait_ge(M["sums_ready"], 8 * n + 8)
            act.wait_ge(M["level_done"], 9 * n + 8)
            F(buf["x"][:, 1], buf["suf"][:, :, :], ACT.Exp)
            F(buf["qd"][:, :, :], buf["pre"][:, :, TP:T], ACT.Exp)
            F(buf["dec"][:, :, :], sample_last(buf["pre"]), ACT.Exp).then_inc(M["kd_exp"], 1)

        def gate_soft(M, buf, n):
            t1, t2 = buf["x"][:, 0], buf["x"][:, 1]
            step(F(t2, t1, ACT.Abs))
            step(F(t2, t2, ACT.Exp, scale=-1.0))
            F(t2, t2, ACT.Ln, bias=ones[:, 0:1]).then_inc(M["gate_log"], 1)

        def head_rstd(M, wait, src, width):
            act.wait_ge(M["summed"], wait)
            step(F(rstd[:, :], src[:, 0:T], ACT.Ln, scale=1.0 / width, bias=eps[:, :]))
            F(rstd[:, :], rstd[:, :], ACT.Exp, scale=-0.5).then_inc(M["rstd_ready"], 1)

        def hg_pair(pn):
            return cols(2 * pn, 2)

        def hg_load(n, h):
            act.dma_start(hg["s0"][:, h], hg_state[cols(2 * n + h, 1)].rearrange("h k b v -> (h k) b v")
                          ).then_inc(H["s0_loaded"][h], 16)

        def hg_step(n, s, own, prev):
            pn = n - 1
            if prev:
                if s in (0, 1):
                    level_exp(H, hg, pn, s + 7)
                elif s == 2:
                    key_exp(H, hg, pn)
                elif s in (4, 5):
                    h = s - 4
                    act.wait_ge(H["turned"], 2 * pn + h + 1)
                    F(hg["tm"][:, h].rearrange("p a c -> p (a c)"), b6[:, :], ACT.Copy).then_inc(H["turned_read"], 1)
                    if h == 0:
                        act.wait_ge(H["s_turned"], pn + 1)
                        F(hg["ts"].rearrange("p a c -> p (a c)"), b7[0:32, :], ACT.Copy).then_inc(H["s_turned_read"], 1)
                elif s in (6, 8):
                    h = (s - 6) // 2
                    act.wait_ge(H["o_done"], 2 * pn + h + 1)
                    if h == 1:
                        act.wait_ge(H["summed"], 2 * pn + 1)
                    F(o_buf[:, cols(2 * pn + h, 1), :].rearrange("p a t -> p (a t)"), b7[:, 0:T], ACT.Copy)
                    F(hg["sq"][:, :], b7[:, 0:T], ACT.Square).then_inc(H["o_read"], 1)
                elif s in (7, 9):
                    h = (s - 7) // 2
                    if h == 1:
                        act.wait_ge(H["o_ready"], 2 * pn + 1)
                    head_rstd(H, 2 * pn + h + 1, b6, P)
                if s == 7:
                    act.wait_ge(H["ps_done"], pn + 1)
                    F(hg["sp"].rearrange("p h v -> p (h v)"), b4[:, 0:256], ACT.Copy).then_inc(H["ps_read"], 1)
                    act.wait_ge(H["ps_read"], pn + 1)
                    act.dma_start(A["new_hgrn_prompt"][0, 0].rearrange("h k v -> k h v")[:, hg_pair(pn), :],
                                  hg["sp"][:, :, :]).then_inc(H["ps_stored"], 16)
                if s in (11, 12):
                    h = s - 11
                    act.wait_ge(H["ss_read"], 4 * pn + 2 * h + 2)
                    act.dma_start(hg_state_out[cols(2 * pn + h, 1)].rearrange("h k b v -> (h k) b v"),
                                  hg["s0"][:, h]).then_inc(H["s0_stored"][h], 16)
                if s == 12:
                    act.wait_ge(H["ps_stored"], 16 * (pn + 1))
                if s == 14 and own:
                    for h in range(2):
                        act.wait_ge(H["s0_stored"][h], 16 * (pn + 1))
                        hg_load(n, h)
            if own:
                if s == 5:
                    if prev:
                        act.wait_ge(H["s_turned"], pn + 1)
                    panel_done(HG, n, 3)
                    t1, t2 = hg["x"][:, 0], hg["x"][:, 1]
                    F(t1, panel(HG, 0), ACT.Copy).then_inc(panel_read["A"], 1)
                    act.wait_ge(panel_read["A"], HG.emptied(n, 0)[1])
                    gate_soft(H, hg, n)
                    act.wait_ge(H["gate_lin"], n + 1)
                    for h in range(2):
                        last = F(hg["k"][:, h], t1[:, h], ACT.Exp, bias=lbv[:, 1, cols(2 * n + h, 1)])
                    last.then_inc(H["k_ready"], 1)
                    act.wait_ge(H["gate_mix"], n + 1)
                    step(F(hg["suf"][:, :, :], hg["suf"][:, :, :], ACT.Exp))
                    F(hg["suf"][:, :, :], hg["suf"][:, :, :], ACT.Ln, bias=ones[:, 0:1]).then_inc(H["gate_soft"], 1)
                elif s == 8:
                    act.wait_ge(ada_used, HG.a0 + KB * (n + 1))
                    if not isinstance(n, int) or n:
                        act.wait_ge(ada_turned, 4 + n)
                    F(hg["ada"][:, :], b5[:, 0:256], ACT.Copy).then_inc(ada_copied, 1)
                    panel_done(HG, n, 7)
                    silu_exp(H, hg["q"][:, :, :], panel(HG, 1))
                elif s == 12:
                    panel_done(HG, n, 11)
                    F(hg["v"][:, :, :], panel(HG, 2), ACT.Copy).then_inc(panel_read["A"], 1)
                if s >= 10:
                    level_exp(H, hg, n, s - 9)

        def hg_iteration(n, prev):
            for s in range(16):
                cast(HG, n, s + AHEAD)
                hg_step(n, s, True, prev)
            panel_done(HG, n, 15)
            if prev:
                act.wait_ge(H["o_ready"], 2 * n)
            silu_exp(H, hg["g"][:, :, :], panel(HG, 3))

        for h in range(2):
            hg_load(0, h)
        hg_iteration(0, False)
        tally.start("hg_act")
        with act.Fori(1, HG_PAIRS) as n:
            tally.at(n, 1)
            hg_iteration(n, True)
        tally.end(HG_PAIRS - 1)

        def out_projection(st, tail):
            act.wait_ge(tile_done, st.w0)
            for s in range(32):
                cast(st, 0, s + AHEAD)
                if s < 3:
                    split_o(s)
                for x in ((2 * s, 2 * s + 1) if s < 5 else (10, 11, 12, 13) if s == 5 else ()):
                    tail(x)
                if s == 5:
                    (act.wait_ge(H["o_ready"], 16) if st is HGO else act.wait_ge(G["o_ready"], GLA_HEADS))
                    split_o(3)

        def out_first(st):
            act.wait_ge(*((H["o_ready"], 14) if st is HGO else (G["o_ready"], GLA_HEADS - 1)))

        out_first(HGO)
        out_projection(HGO, lambda s: hg_step(HG_PAIRS, s, False, True))

        def layer_norm(i, e):
            for c in range(4):
                act.wait_ge(ln_centered, 4 * i + c + 1)
                F(ln["sq"][:, 4 * c:4 * c + 4, :], z[:, 4 * c:4 * c + 4, :], ACT.Square).then_inc(ln_squared, 1)
            act.wait_ge(ln_var, i + 1)
            step(F(rstd[:, :], b5[:, 0:T], ACT.Ln, scale=1.0 / D, bias=eps[:, :]))
            F(rstd[:, :], rstd[:, :], ACT.Exp, scale=-0.5).then_inc(ln_rstd, 1)
            if e is not None:
                split_h(e, i + 1, ln_scaled, 4 * i)

        def mlp(st, e, n, with_ada, last_n=False):
            for s in range(64):
                if not (last_n and s + AHEAD >= 64):
                    cast(st, n, s + AHEAD)
                if s % 4 == 0 and 4 <= s <= 32:
                    p = s // 4 - 1
                    panel_done(st, n, s - 1)
                    r = mlp_b["r"][:, p % 2]
                    if p >= 2:
                        act.wait_ge(act_ready, act_base[e] + 8 * n + p - 1)
                    F(r, panel(st, p), ACT.Relu).then_inc(panel_read["A"], 1)
                    act.wait_ge(panel_read["A"], st.emptied(n, p)[1])
                    F(act_hi[:, 2 * p:2 * p + 2, :], r, ACT.Square).then_inc(act_high, 1)
                if with_ada and s == 49:
                    act.wait_ge(ada_used, st.a0 + 48 * (n + 1))
                    act.wait_ge(ada_turned, 12 + n)
                    F(mlp_b["ada"][:, 0:512], b4[:, :], ACT.Copy)
                    F(mlp_b["ada"][:, 512:768], b5[:, 0:256], ACT.Copy).then_inc(ada_copied, 1)

        layer_norm(0, 2)
        with act.Fori(0, MLP0.iters) as n:
            mlp(MLP0, 2, n, True)
        layer_norm(1, 3)

        def gl_load(n, b):
            act.dma_start(gl["s0"][:, b % 4], gl_state[cols(n, 1), b].rearrange("h k j v -> (h k) j v")
                          ).then_inc(G["s0_loaded"][b % 4], 16)

        def gl_store(n, b):
            act.wait_ge(G["ss_read"], 8 * n + b + 1)
            act.dma_start(gl_state_out[cols(n, 1), b].rearrange("h k j v -> (h k) j v"), gl["s0"][:, b % 4]
                          ).then_inc(G["s0_stored"][b % 4], 16)

        def gl_reload(n, b, nxt):
            if b >= 4 and nxt is None:
                return
            act.wait_ge(G["s0_stored"][b % 4], 32 * n + 16 * (b // 4 + 1))
            gl_load(*((n, b + 4) if b < 4 else (nxt, b - 4)))

        def gl_state_copy(n, j):
            act.wait_ge(G["ps_done"], 2 * n + j + 1)
            F(gl["sp"][:, :], b6[:, :], ACT.Copy).then_inc(G["ps_read"], 1)
            act.wait_ge(G["ps_read"], 2 * n + j + 1)
            act.dma_start(A["new_gla_prompt"][0, 0].rearrange("h (j k) v -> h k j v", j=2)[cols(n, 1), :, j, :]
                          .rearrange("h k v -> (h k) v"), gl["sp"][:, :]).then_inc(G["ps_stored"], 16)

        def gl_step(n, s, own, prev):
            pn = n - 1
            if prev:
                if s == 1:
                    act.wait_ge(G["ps_stored"], 16 * (2 * pn + 1))
                    gl_state_copy(pn, 1)
                if s <= 7:
                    gl_store(pn, s)
                if 1 <= s <= 8:
                    gl_reload(pn, s - 1, n if own else None)
                if s == 7:
                    act.wait_ge(G["oi_done"], pn + 1)
                    F(o_buf[:, cols(4 * pn, 4), TP:T], b7[:, 0:128].rearrange("p (v t) -> p v t", v=4), ACT.Copy
                      ).then_inc(G["oi_read"], 1)
                for v, at in enumerate((7, 9, 9, 10)):
                    if s == at:
                        act.wait_ge(G["o_done"], 4 * pn + v + 1)
                        F(o_buf[:, cols(4 * pn + v, 1), 0:TP].rearrange("p a t -> p (a t)"), (b6, b7)[v % 2][:, 0:TP],
                          ACT.Copy).then_inc(G["o_read"], 1)
                if s == 10:
                    act.wait_ge(G["att_set"], 1)
                    act.wait_ge(G["o_read"], 4 * pn + 4)
                    F(gl["v"][:, :, :], o_buf[:, cols(4 * pn, 4), :], ACT.Square).then_inc(G["squared"], 1)
                if s == 11:
                    head_rstd(G, pn + 1, b5, GLA_V)
            if own:
                if s == 0:
                    if prev:
                        act.wait_ge(G["gk_done"], 2 * n)
                    act.dma_start(gl["gk2"][P - GLA_RANK:P], A["gla_w_gk2"][0].rearrange("r (a c) -> r a c", c=P)
                                  [:, cols(2 * n, 2), :]).then_inc(G["gk2_loaded"], 16)
                if s in (3, 5):
                    j = (s - 3) // 2
                    act.wait_ge(G["gk_done"], 2 * n + j + 1)
                    F(gl["x"][:, 0, j], b6[:, 0:T], ACT.Identity, bias=vec[:, cols(48 + 2 * n + j, 1)]
                      ).then_inc(G["gk_read"], 1)
                if s == 5:
                    act.wait_ge(G["gk_read"], 2 * n + 2)
                    gate_soft(G, gl, n)
                    panel_done(GLA, n, 3)
                    F(gl["q"][:, :, :], panel(GLA, 0), ACT.Copy, scale=GLA_K ** -0.5).then_inc(panel_read["A"], 1)
                elif s == 8:
                    panel_done(GLA, n, 7)
                    F(gl["k"][:, :, :], panel(GLA, 1), ACT.Copy).then_inc(panel_read["A"], 1)
                elif s in (12, 16):
                    j = (s - 12) // 4
                    panel_done(GLA, n, s - 1)
                    F(gl["v"][:, 2 * j:2 * j + 2, :], panel(GLA, 2 + j), ACT.Copy).then_inc(panel_read["A"], 1)
                elif s == 20:
                    panel_done(GLA, n, 19)
                    silu_exp(G, gl["g"][:, 0:2, :], panel(GLA, 4))
                if 11 <= s <= 18:
                    level_exp(G, gl, n, s - 10)
                if s == 18:
                    for t in range(2):
                        act.wait_ge(G["turned"], 3 * n + t + 1)
                        F(gl["vt"][:, t, :], (b6, b7)[t][:, :], ACT.Copy).then_inc(G["turned_read"], 1)
                elif s == 19:
                    key_exp(G, gl, n)
                elif s == 20:
                    act.wait_ge(G["s_turned"], 2 * n + 1)
                    F(gl["vs"][:, :], b6[0:32, :], ACT.Copy).then_inc(G["s_turned_read"], 1)
                elif s == 21:
                    act.wait_ge(G["turned"], 3 * n + 3)
                    F(gl["kt"].rearrange("p t j c -> p (t j c)"), b5[:, :], ACT.Copy).then_inc(G["turned_read"], 1)
                    act.wait_ge(G["s_turned"], 2 * n + 2)
                    F(gl["ks"].rearrange("p j c -> p (j c)"), b7[0:32, 0:256], ACT.Copy).then_inc(G["s_turned_read"], 1)
                elif s == 23:
                    if prev:
                        act.wait_ge(G["ps_stored"], 32 * n)
                    gl_state_copy(n, 0)

        def gl_iteration(n, prev):
            for s in range(24):
                cast(GLA, n, s + AHEAD)
                gl_step(n, s, True, prev)
            panel_done(GLA, n, 23)
            silu_exp(G, gl["g"][:, 2:4, :], panel(GLA, 5))

        act.wait_ge(G["gk2_set"], 1)
        for b in range(4):
            gl_load(0, b)
        for s in range(4):
            cast(LOW, 0, s + AHEAD)
        panel_done(LOW, 0, 3)
        F(gl["low"][:, :], main[:, LOW.bank(0) + 1, 0:T], ACT.Copy).then_inc(panel_read["A"], 1)
        gl_iteration(0, False)
        tally.start("gl_act")
        with act.Fori(1, GLA_HEADS) as n:
            tally.at(n, 1)
            gl_iteration(n, True)
        tally.end(GLA_HEADS - 1)
        out_first(GLO)
        out_projection(GLO, lambda s: gl_step(GLA_HEADS, s, False, True))
        layer_norm(2, 5)
        with act.Fori(0, MLP1.iters - 1) as n:
            mlp(MLP1, 5, n, False)
        mlp(MLP1, 5, MLP1.iters - 1, False, last_n=True)
        layer_norm(3, None)
        for i in range(3):
            r = P if i < 2 else TS
            for c in range(4):
                g = 4 * i + c
                act.wait_ge(y_turned, g + 1)
                F(yout[0:r, i, c * 512:(c + 1) * 512], main[0:r, g % 4, :], ACT.Copy).then_inc(y_read, 1)
            act.wait_ge(y_read, 4 * i + 4)
            dst = (A["y_prompt"][0, 0:P, :], A["y_prompt"][0, P:TP, :], A["y_sample"].rearrange("b t d -> (b t) d"))[i]
            act.dma_start(dst, yout[0:r, i, :]).then_inc(y_stored, 16)

    @block.vector
    def _(dve):
        tally = Tally(dve, dve_step)
        step = tally.step
        V = nc.vector

        def split(st, n, g):
            slot, _ = st.ring(n, "w", g)
            dve.wait_ge(hi_ready, st.tile(n, g) + 1)
            s = st.split_slot(g)
            V.tensor_tensor(w_lo[:, s].rearrange("p k n -> p (k n)"), raw[:, slot, :],
                            w_hi[:, s].rearrange("p k n -> p (k n)").bitcast(F32), ALU.subtract).then_inc(lo_ready, 1)

        def low_part(e, c, src):
            dve.wait_ge(a_high, 4 * e + c + 1)
            V.tensor_tensor(a_lo[:, 4 * c:4 * c + 4, :], src, a_hi[:, 4 * c:4 * c + 4, :].bitcast(F32),
                            ALU.subtract).then_inc(a_ready, 1)

        def sample_h(c):
            k = slice(4 * c, 4 * c + 4)
            h = seqs(ln["h"][:, c % 2, :, TP:T])
            step(V.tensor_tensor(h, seqs(z[:, k, TP:T]), per_token(c1[:, k, 1:NSEQ]), ALU.mult))
            V.tensor_tensor(h, h, per_token(c0[:, k, 1:NSEQ]), ALU.add).then_inc(a_sample, 1)

        def mod_update(layer, block0, groups, count, src):
            dve.wait_ge(ada_turned, count)
            for i in range(groups):
                out = mod[:, layer, cols(block0 + 8 * i, 8), :].rearrange("p (j s) q -> p s j q", s=2)
                bias = b_ada[:, layer, cols(block0 + 8 * i, 8)].rearrange("p (j s) -> p s j", s=2)
                for s_ in range(2):
                    ps = src[i][:, s_ * P:(s_ + 1) * P].rearrange("p (j q) -> p j q", q=32)[:, :, 0:NSEQ]
                    last = V.tensor_tensor(out[:, s_], ps, bias[:, s_].unsqueeze(2).to_broadcast([P, 4, NSEQ]), ALU.add)
            last.then_inc(mod_ready, 1)

        dve.wait_ge(boot_loaded, 16 * BOOT_LOADS)
        step(V.memset(c_t[:, :, :], 0.0))
        step(V.tensor_copy(masks[:, :, :], boot["masks"][:, :, :]))
        dve.wait_ge(boot_turned, 1)
        for layer in range(2):
            last = V.tensor_copy(b_ada[:, layer, :], main[:, 0, 96 * layer:96 * layer + 96])
        last.then_inc(boot_read, 1)
        dve.wait_ge(boot_read, 1)
        V.tensor_scalar(b_ada[:, :, KB:3 * KB], b_ada[:, :, KB:3 * KB], 1.0, None, ALU.add)
        step(V.tensor_scalar(b_ada[:, :, 4 * KB:6 * KB], b_ada[:, :, 4 * KB:6 * KB], 1.0, None, ALU.add))
        dve.wait_ge(boot_turned, 2)
        V.tensor_copy(lnv.rearrange("p a l i k -> p (a l i k)"), main[:, 1, 0:P])
        V.tensor_copy(vec[:, :], main[:, 1, P:P + 56]).then_inc(boot_read, 1)
        dve.wait_ge(boot_turned, 3)
        V.tensor_copy(boot["c_f"].rearrange("p k q -> p (k q)"), main[:, 2, 0:KB * NSEQ]).then_inc(boot_read, 1)
        dve.wait_ge(c_exp, 1)
        ce = boot["c_e"][:, :, :]
        step(V.tensor_scalar(ce, ce, 1.0, None, ALU.add))
        step(V.reciprocal(ce, ce))
        V.tensor_tensor(c_t[:, :, 0:NSEQ], boot["c_f"][:, :, :], ce, ALU.mult).then_inc(c_ready, 1)
        step(V.tensor_tensor(lbv[:, 1, :], vec[:, 0:KB], vec[:, 0:KB], ALU.max))
        V.tensor_tensor(lbv[:, 0, :], vec[:, 0:KB], lbv[:, 1, :], ALU.subtract).then_inc(lb_ready, 1)
        dve.wait_ge(lb_exp, 1)
        step(V.reciprocal(lbv[:, 1, :], lbv[:, 0, :]))
        step(V.tensor_tensor(lbv[:, 0, :], lbv[:, 0, :], lbv[:, 1, :], ALU.mult))
        step(V.tensor_tensor(lbv[:, 1, :], lbv[:, 0, :], lbv[:, 0, :], ALU.subtract))
        step(V.tensor_scalar(lbv[:, 0, :], lbv[:, 1, :], 0.0, 1.0 - 1e-6, ALU.max, ALU.min))
        V.tensor_scalar(lbv[:, 3, :], lbv[:, 0, :], LB_LEAST, None, ALU.max).then_inc(lb_ready, 1)
        dve.wait_ge(lb_logs, 1)
        step(V.tensor_scalar(lbv[:, 3, :], lbv[:, 0, :], LB_LEAST, -1e30, ALU.is_lt, ALU.mult))
        step(V.tensor_tensor(lbv[:, 2, :], lbv[:, 2, :], lbv[:, 3, :], ALU.add))
        for i in range(3):
            r = P if i < 2 else TS
            for c in range(4):
                g = 3 + 4 * i + c
                dve.wait_ge(boot_turned, g + 1)
                V.tensor_scalar(z[:, 4 * c:4 * c + 4, i * P:i * P + r],
                                main[:, g % 4, 0:4 * r].rearrange("p (k t) -> p k t", k=4), ALPHA, None, ALU.mult
                                ).then_inc(boot_read, 1)
        for n in range(4):
            mod_update(0, 8 * n, 1, n + 1, [b7])
        dve.wait_ge(mod_ready, 4)
        V.tensor_scalar(c1[:, :, :], mod[:, 0, KB:2 * KB, :], 1.0 / ALPHA, None, ALU.mult)
        V.tensor_copy(c0[:, :, :], mod[:, 0, 0:KB, :]).then_inc(h_terms, 1)
        for g in range(AHEAD):
            split(HG, 0, g)
        dve.wait_ge(h_terms, 1)
        for c in range(4):
            if c >= 2:
                dve.wait_ge(a_ready, c - 1)
            sample_h(c)
            low_part(0, c, ln["h"][:, c % 2])
        dve.wait_ge(a_ready, 4)
        V.memset(hg["att"][:, :, :, :], 0.0).then_inc(H["att_set"], 1)
        V.memset(hg["atts"][:, :, :], 0.0).then_inc(H["att_set"], 1)

        def silu(M, count, x, src):
            dve.wait_ge(M["silu_exp"], count)
            step(V.tensor_scalar(x, x, 1.0, None, ALU.add))
            step(V.reciprocal(x, x))
            V.tensor_tensor(x, x, src, ALU.mult).then_inc(panel_read["V"], 1)

        def level_mul(M, buf, n, L):
            dve.wait_ge(M["exp_ready"], 8 * n + L)
            x = buf["x"][:, L % 2]
            for second, src in ((False, buf["k"]), (True, buf["q"])):
                xs = halves(x, L, second)
                last = V.tensor_tensor(xs, xs, halves(src, L, second), ALU.mult)
            last.then_inc(M["level_ready"], 1)

        def hg_read(n, L, prev):
            if L == 0 and prev:
                dve.wait_ge(H["o_done"], 2 * n)
            in_register(dve, 9 * n + L, 9 * n + L + 1)
            dve.wait_ge(H["att_set"], 2)
            if L:
                dve.wait_ge(H["level_read"], 9 * n + L)
            dve.wait_ge(H["level_done"], 9 * n + L + 1)
            bank = b4 if L % 2 == 0 else b5
            if L <= 2:
                V.copy_predicated(hg["atts"][:, :, :], level_mask(L, 2, 32),
                                  b6[0:32, 64 * L:64 * L + 64].rearrange("p (h t) -> p h t", h=2))
            if L == 8:
                V.tensor_copy(hg["att"][:, :, 1, :], bank[:, 0:256].rearrange("p (h t) -> p h t", h=2)
                              ).then_inc(H["level_read"], 1)
            else:
                for h in range(2):
                    last = V.copy_predicated(hg["att"][:, h, 0:3:2, :], level_mask(L, 2),
                                             bank[:, 256 * h:256 * h + 256].rearrange("p (a t) -> p a t", a=2))
                last.then_inc(H["level_read"], 1)

        def key_mul(M, buf, n):
            dve.wait_ge(M["kd_exp"], n + 1)
            V.tensor_tensor(buf["x"][:, 1], buf["x"][:, 1], buf["k"][:, :, :], ALU.mult)
            V.tensor_tensor(buf["qd"][:, :, :], buf["qd"][:, :, :], buf["q"][:, :, TP:T], ALU.mult
                            ).then_inc(M["kd_ready"], 1)

        def hg_step(n, s, own, prev):
            pn = n - 1
            if prev:
                if s in (0, 1):
                    level_mul(H, hg, pn, s + 7)
                if s <= 3:
                    hg_read(pn, s + 5, True)
                if s == 2:
                    key_mul(H, hg, pn)
                if s == 5:
                    dve.wait_ge(H["s_turned_read"], pn + 1)
                    for h in range(2):
                        V.tensor_tensor(hg["vsm"][:, h], hg["ts"][:, h, :].unsqueeze(1).to_broadcast([32, NB, P]),
                                        bmask[0:32, :].unsqueeze(2).to_broadcast([32, NB, P]), ALU.mult
                                        ).then_inc(H["s_masked"], 1)
                for x, at in enumerate((9, 10, 10, 11)):
                    if s == at:
                        h = x // 2
                        dve.wait_ge(H["ss_done"], 4 * pn + x + 1)
                        for i in range(4):
                            b = 4 * (x % 2) + i
                            last = V.scalar_tensor_tensor(
                                out=hg["s0"][:, h, b, :], in0=hg["s0"][:, h, b, :], scalar=hg["dec"][:, h, b:b + 1],
                                in1=(b4, b7, b5, b7)[x][:, i * P:(i + 1) * P], op0=ALU.mult, op1=ALU.add)
                        last.then_inc(H["ss_read"], 1)
                if s in (8, 10):
                    h = (s - 8) // 2
                    dve.wait_ge(H["rstd_ready"], 2 * pn + h + 1)
                    o = o_buf[:, cols(2 * pn + h, 1), :].rearrange("p a t -> p (a t)")
                    step(V.tensor_tensor(o, o, rstd[:, :], ALU.mult))
                    V.scalar_tensor_tensor(out=o, in0=o, scalar=vec[:, cols(KB + 2 * pn + h, 1)], in1=hg["g"][:, h],
                                           op0=ALU.mult, op1=ALU.mult).then_inc(H["o_ready"], 1)
            if own:
                if s == 5:
                    t1, t2, pre, suf = hg["x"][:, 0], hg["x"][:, 1], hg["pre"], hg["suf"]
                    dve.wait_ge(H["gate_log"], n + 1)
                    step(V.scalar_tensor_tensor(out=pre[:, :, :], in0=t1, scalar=0.0, in1=t2, op0=ALU.min,
                                                op1=ALU.subtract))
                    V.tensor_tensor(t1, pre[:, :, :], t1, ALU.subtract).then_inc(H["gate_lin"], 1)
                    for h in range(2):
                        last = V.tensor_scalar(t2[:, h], pre[:, h], lbv[:, 1, cols(2 * n + h, 1)], None, ALU.add)
                    step(last)
                    for h in range(2):
                        last = V.tensor_scalar(pre[:, h], t2[:, h], lbv[:, 2, cols(2 * n + h, 1)], None, ALU.max)
                    step(last)
                    for h in range(2):
                        last = V.scalar_tensor_tensor(out=suf[:, h], in0=t2[:, h], scalar=lbv[:, 2, cols(2 * n + h, 1)],
                                                      in1=pre[:, h], op0=ALU.min, op1=ALU.subtract)
                    last.then_inc(H["gate_mix"], 1)
                elif s == 6:
                    dve.wait_ge(H["gate_soft"], n + 1)
                    step(V.tensor_tensor(hg["pre"][:, :, :], hg["pre"][:, :, :], hg["suf"][:, :, :], ALU.add))
                    V.memset(hg["suf"][:, :, :], 0.0).then_inc(H["gates_ready"], 1)
                elif s == 9:
                    silu(H, 2 * n + 1, hg["q"][:, :, :], panel(HG, 1))
                    dve.wait_ge(panel_read["V"], HG.emptied(n, 1)[1])
                if s >= 10:
                    level_mul(H, hg, n, s - 9)
                if s >= 11:
                    hg_read(n, s - 11, prev)
                if s == 13:
                    mod_update(0, 8 * n + 2 * KB, 1, 5 + n, [b7])

        def hg_iteration(n, prev):
            for s in range(16):
                split(HG, n, s + AHEAD)
                hg_step(n, s, True, prev)
            silu(H, 2 * n + 2, hg["g"][:, :, :], panel(HG, 3))
            dve.wait_ge(panel_read["V"], HG.emptied(n, 3)[1])

        hg_iteration(0, False)
        tally.start("hg_dve")
        with dve.Fori(1, HG_PAIRS) as n:
            tally.at(n, 1)
            hg_iteration(n, True)
        tally.end(HG_PAIRS - 1)

        def residual(st, n, p, layer, gate, j):
            src, zs = panel(st, p), mlp_b["zs"]
            for i in range(2):
                kb = 2 * j + i
                V.scalar_tensor_tensor(out=z[:, kb, 0:TP], in0=src[:, i, 0:TP], scalar=mod[:, layer, gate * KB + kb, 0:1],
                                       in1=z[:, kb, 0:TP], op0=ALU.mult, op1=ALU.add)
            k = slice(gate * KB + 2 * j, gate * KB + 2 * j + 2)
            V.tensor_tensor(seqs(zs[:, :, :]), seqs(src[:, :, TP:T]), per_token(mod[:, layer, k, 1:NSEQ]), ALU.mult
                            ).then_inc(panel_read["V"], 1)
            dve.wait_ge(panel_read["V"], st.emptied(n, p)[1])
            zk = z[:, 2 * j:2 * j + 2, TP:T]
            step(V.tensor_tensor(zk, zk, zs[:, :, :], ALU.add))

        def out_projection(st, tail, e, layer):
            for s in range(32):
                split(st, 0, s + AHEAD)
                if s < 3:
                    low_part(e, s, o_buf[:, 4 * s:4 * s + 4, :])
                for x in ((2 * s, 2 * s + 1) if s < 5 else (10, 11, 12, 13) if s == 5 else ()):
                    tail(x)
                if s == 5:
                    low_part(e, 3, o_buf[:, 12:16, :])
                if s and s - 1 in OUT_DONE:
                    p = OUT_DONE.index(s - 1)
                    dve.wait_ge(tile_done, st.tile(0, s - 1) + 1)
                    residual(st, 0, p, layer, 2, p)
            dve.wait_ge(tile_done, st.tile(0, 31) + 1)
            residual(st, 0, 7, layer, 2, 7)

        out_projection(HGO, lambda s: hg_step(HG_PAIRS, s, False, True), 1, 0)

        def layer_norm(i, e):
            layer, which = divmod(i, 2)
            w, b = lnv[:, 0, layer, which, :], lnv[:, 1, layer, which, :]
            V.tensor_reduce(mu[:, :], z.rearrange("p k t -> p t k"), AX.X, ALU.add).then_inc(ln_sum, 1)
            if e is not None:
                nl, shift, _ = LAYER_MOD[i + 1] if i < 3 else (0, 0, 0)
                sc = mod[:, nl, (shift + 1) * KB:(shift + 2) * KB, :]
                sh = mod[:, nl, shift * KB:(shift + 1) * KB, :]
                step(V.tensor_tensor(c1[:, :, :], sc, per_seq(w), ALU.mult))
                step(V.tensor_tensor(c0[:, :, :], sc, per_seq(b), ALU.mult))
                step(V.tensor_tensor(c0[:, :, :], c0[:, :, :], sh, ALU.add))
                V.tensor_scalar(awb[:, 0, :], w, ALPHA, None, ALU.mult)
                step(V.tensor_scalar(awb[:, 1, :], b, ALPHA, None, ALU.mult))
            dve.wait_ge(ln_mean, i + 1)
            step(V.tensor_scalar(mu[:, :], b4[:, 0:T], 1.0 / D, None, ALU.mult))
            for c in range(4):
                zc = z[:, 4 * c:4 * c + 4, :]
                V.tensor_tensor(zc, zc, mu[:, :].unsqueeze(1).to_broadcast([P, 4, T]), ALU.subtract
                                ).then_inc(ln_centered, 1)
            dve.wait_ge(ln_rstd, i + 1)

            def scale(c):
                zc = z[:, 4 * c:4 * c + 4, :]
                V.tensor_tensor(zc, zc, rstd[:, :].unsqueeze(1).to_broadcast([P, 4, T]), ALU.mult
                                ).then_inc(ln_scaled, 1)

            def affine(c, wv, bv):
                for kb in range(4 * c, 4 * c + 4):
                    last = V.tensor_scalar(z[:, kb, :], z[:, kb, :], wv[:, kb:kb + 1], bv[:, kb:kb + 1], ALU.mult, ALU.add)
                return last

            if e is None:
                for c in range(4):
                    scale(c)
                    dve.wait_ge(ln_scaled, 4 * i + c + 1)
                    affine(c, w, b).then_inc(y_ready, 1)
                return
            scale(0)
            for c in range(4):
                if c < 3:
                    scale(c + 1)
                if c >= 2:
                    dve.wait_ge(a_ready, 4 * e + c - 1)
                dve.wait_ge(ln_scaled, 4 * i + c + 1)
                sample_h(c)
                low_part(e, c, ln["h"][:, c % 2])
            for c in range(4):
                last = affine(c, awb[:, 0, :], awb[:, 1, :])
            step(last)

        def mlp(st, e, n, layer, with_ada, last_n=False):
            for s in range(64):
                if not (last_n and s + AHEAD >= 64):
                    split(st, n, s + AHEAD)
                if s % 4 == 0 and 4 <= s <= 32:
                    p = s // 4 - 1
                    r = mlp_b["r"][:, p % 2]
                    dve.wait_ge(act_high, act_base[e] + 8 * n + p + 1)
                    step(V.tensor_tensor(r, r, r, ALU.mult))
                    V.tensor_tensor(act_lo[:, 2 * p:2 * p + 2, :], r, act_hi[:, 2 * p:2 * p + 2, :].bitcast(F32),
                                    ALU.subtract).then_inc(act_ready, 1)
                if s % 4 == 0 and s > 32:
                    dve.wait_ge(tile_done, st.tile(n, s - 1) + 1)
                    residual(st, n, s // 4 - 1, layer, 5, s // 4 - 9)
                if with_ada and s == 54:
                    mod_update(1, 24 * n, 3, 13 + n, [b6[:, 0:256], b6[:, 256:512], b7[:, 0:256]])
            dve.wait_ge(tile_done, st.tile(n, 63) + 1)
            residual(st, n, 15, layer, 5, 7)

        layer_norm(0, 2)
        tally.start("mlp0_dve")
        with dve.Fori(0, MLP0.iters) as n:
            tally.at(n, 0)
            mlp(MLP0, 2, n, 0, True)
        tally.end(MLP0.iters)
        layer_norm(1, 3)

        def gl_read(n, L, prev):
            if L == 0 and prev:
                dve.wait_ge(G["o_done"], 4 * n)
            in_register(dve, 9 * n + L, 9 * n + L + 1)
            dve.wait_ge(G["att_set"], 2)
            if L:
                dve.wait_ge(G["level_read"], 9 * n + L)
            dve.wait_ge(G["level_done"], 9 * n + L + 1)
            bank = b4 if L % 2 == 0 else b5
            if L <= 2:
                V.copy_predicated(gl["atts"][:, :], masks[0:32, L, 0:32], b6[0:32, 32 * L:32 * L + 32])
            if L == 8:
                V.tensor_copy(gl["att"][:, 1, :], bank[:, 0:P]).then_inc(G["level_read"], 1)
            else:
                V.copy_predicated(gl["att"][:, 0:3:2, :], level_mask(L, 2),
                                  bank[:, 0:256].rearrange("p (a t) -> p a t", a=2)).then_inc(G["level_read"], 1)

        def gl_mask(n, b):
            if b >= 2:
                dve.wait_ge(G["ss_done"], 8 * n + b - 1)
            V.tensor_scalar(gl["ksm"][:, b % 2], gl["ks"][:, :, :], bmask[0:32, b:b + 1], None, ALU.mult
                            ).then_inc(G["s_masked"], 1)

        def gl_state(n, b):
            dve.wait_ge(G["ss_done"], 8 * n + b + 1)
            for j, bank in enumerate((b4, b5)):
                s0 = gl["s0"][:, b % 4, j, :]
                last = V.scalar_tensor_tensor(out=s0, in0=s0, scalar=gl["dec"][:, j, b:b + 1], in1=bank[:, :],
                                              op0=ALU.mult, op1=ALU.add)
            last.then_inc(G["ss_read"], 1)

        def gl_step(n, s, own, prev):
            pn = n - 1
            if prev:
                if s <= 7:
                    gl_state(pn, s)
                if s <= 5:
                    gl_mask(pn, s + 2)
                if s == 12:
                    dve.wait_ge(G["rstd_ready"], pn + 1)
                    o = o_buf[:, cols(4 * pn, 4), :]
                    step(V.tensor_tensor(o, o, rstd[:, :].unsqueeze(1).to_broadcast([P, 4, T]), ALU.mult))
                    for v in range(4):
                        o = o_buf[:, cols(4 * pn + v, 1), :].rearrange("p a t -> p (a t)")
                        last = V.scalar_tensor_tensor(out=o, in0=o, scalar=vec[:, cols(2 * KB + 4 * pn + v, 1)],
                                                      in1=gl["g"][:, v], op0=ALU.mult, op1=ALU.mult)
                    last.then_inc(G["o_ready"], 1)
            if own:
                if s == 6:
                    t1, t2, pre = gl["x"][:, 0], gl["x"][:, 1], gl["pre"][:, :, :]
                    dve.wait_ge(G["gate_log"], n + 1)
                    step(V.scalar_tensor_tensor(out=pre, in0=t1, scalar=0.0, in1=t2, op0=ALU.min, op1=ALU.subtract))
                    step(V.tensor_scalar(pre, pre, 1.0 / GATE_NORM, None, ALU.mult))
                    V.memset(gl["suf"][:, :, :], 0.0).then_inc(G["gates_ready"], 1)
                if 11 <= s <= 18:
                    level_mul(G, gl, n, s - 10)
                if 12 <= s <= 20:
                    gl_read(n, s - 12, prev)
                if s == 19:
                    key_mul(G, gl, n)
                elif s == 21:
                    silu(G, 2 * n + 1, gl["g"][:, 0:2, :], panel(GLA, 4))
                elif s == 22:
                    dve.wait_ge(G["s_turned_read"], 2 * n + 2)
                    if prev:
                        dve.wait_ge(G["ss_done"], 8 * n)
                    gl_mask(n, 0)
                    gl_mask(n, 1)

        def gl_iteration(n, prev):
            for s in range(24):
                split(GLA, n, s + AHEAD)
                gl_step(n, s, True, prev)
            silu(G, 2 * n + 2, gl["g"][:, 2:4, :], panel(GLA, 5))
            dve.wait_ge(panel_read["V"], GLA.emptied(n, 5)[1])

        V.memset(gl["gk2"][:, :, :], 0.0).then_inc(G["gk2_set"], 1)
        V.memset(gl["att"][:, :, :], 0.0).then_inc(G["att_set"], 1)
        V.memset(gl["atts"][:, :], 0.0).then_inc(G["att_set"], 1)
        for s in range(4):
            split(LOW, 0, s + AHEAD)
        gl_iteration(0, False)
        tally.start("gl_dve")
        with dve.Fori(1, GLA_HEADS) as n:
            tally.at(n, 1)
            gl_iteration(n, True)
        tally.end(GLA_HEADS - 1)
        out_projection(GLO, lambda s: gl_step(GLA_HEADS, s, False, True), 4, 1)
        layer_norm(2, 5)
        tally.start("mlp1_dve")
        with dve.Fori(0, MLP1.iters - 1) as n:
            tally.at(n, 0)
            mlp(MLP1, 5, n, 1, False)
        tally.end(MLP1.iters - 1)
        mlp(MLP1, 5, MLP1.iters - 1, 1, False, last_n=True)
        layer_norm(3, None)

    @block.gpsimd
    def _(pool):
        nc.gpsimd.memset(ones[:, :], 1.0)
        nc.gpsimd.memset(eps[:, :], EPS).then_inc(boot_set, 1)

        def sums(M, buf, n, steps_before):
            for L in range(1, 9):
                pool.wait_ge(M["exp_ready"], 8 * n + L)
                pre1, pre2 = (halves(buf["pre"], L, second) for second in (False, True))
                suf1 = halves(buf["suf"], L, False)
                nc.gpsimd.tensor_tensor(suf1, suf1, last_of(pre2), ALU.add).then_inc(pool_step, 1)
                pool.wait_ge(pool_step, steps_before + 8 * n + L)
                nc.gpsimd.tensor_tensor(pre2, pre2, last_of(pre1), ALU.add).then_inc(M["sums_ready"], 1)

        with pool.Fori(0, HG_PAIRS) as n:
            sums(H, hg, n, 0)
        with pool.Fori(0, GLA_HEADS) as n:
            sums(G, gl, n, 8 * HG_PAIRS)

    block.__exit__(None, None, None)


STEPS = {"hg_act": 5, "hg_dve": 10, "gl_act": 3, "gl_dve": 7, "mlp0_dve": 16, "mlp1_dve": 16}
BOOT_LOADS = 16


class Tally:

    def __init__(self, engine, sem):
        self.engine, self.sem, self.count, self.turn = engine, sem, 0, 0

    def step(self, instruction):
        self.count += 1
        instruction.then_inc(self.sem, 1)
        self.engine.wait_ge(self.sem, self.count + self.turn)

    def start(self, name):
        self.name, self.before = name, self.count

    def at(self, n, first):
        self.turn = n * STEPS[self.name] - first * STEPS[self.name]

    def end(self, iterations):
        assert self.count - self.before == STEPS[self.name], (self.name, self.count - self.before)
        self.count, self.turn = self.before + iterations * STEPS[self.name], 0


INPUTS = ["x_prompt", "x_sample", "state_hgrn", "state_gla", "c_prompt", "c_sample", "w_ada", "b_ada", "ln_w", "ln_b",
          "hg_w_in", "hg_lb_raw", "hg_norm_w", "hg_w_out", "gla_w_in", "gla_w_gk2", "gla_b_gk", "gla_norm_w",
          "gla_w_out", "w_up", "w_down"]
OUTPUTS = [("y_prompt", (1, TP, D)), ("y_sample", (NB, TB, D)), ("new_hgrn_prompt", (1, 1, 16, P, P)),
           ("new_gla_prompt", (1, 1, GLA_HEADS, GLA_K, GLA_V)), ("new_hgrn_sample", (1, NB, 16, P, P)),
           ("new_gla_sample", (1, NB, GLA_HEADS, GLA_K, GLA_V))]


def shape_constants():
    s, t = np.arange(P)[:, None], np.arange(P)[None, :]
    masks = np.zeros((P, 8, P), np.float32)
    masks[:, 0] = s == t
    for L in range(1, 8):
        m = 1 << (L - 1)
        masks[:, L] = (s // (2 * m) == t // (2 * m)) & (s // m % 2 == 0) & (t // m % 2 == 1)
    bmask = (np.arange(P)[:, None] // TB == np.arange(NB)[None, :]).astype(np.float32)
    return {"const_ident": np.eye(P, dtype=np.float32), "const_masks": masks, "const_bmask": bmask}


def kernel(**inputs):
    import concourse.bacc as _bacc
    from concourse.bass_utils import run_bass_kernel_spmd as _run

    nc = _bacc.Bacc("TRN2", target_bir_lowering=False, num_devices=1)
    arrays = {f"in_{name}": np.ascontiguousarray(inputs[name]) for name in INPUTS}
    arrays.update({f"in_{name}": a for name, a in shape_constants().items()})
    args = {}
    for name, a in arrays.items():
        args[name[3:]] = nc.dram_tensor(name, a.shape, mybir.dt.from_np(a.dtype), kind="ExternalInput").ap()
    for name, shape in OUTPUTS:
        args[name] = nc.dram_tensor(f"out_{name}", shape, F32, kind="ExternalOutput").ap()
    build_program(nc, args)
    r = _run(nc, [arrays], core_ids=[0])
    return tuple(r.results[0][f"out_{name}"] for name, _ in OUTPUTS)
```

```python
import numpy as np

import concourse.bass as bass
from concourse import mybir

F32 = mybir.dt.float32
F32R = mybir.dt.float32r
U8 = mybir.dt.uint8
ALU = mybir.AluOpType
ACT = mybir.ActivationFunctionType

P = 128
D = 2048
KB = D // P
TP, NB, TB = 256, 8, 4
TS = NB * TB
T = TP + TS
NSEQ = 1 + NB
DEPTH = 2
FF = 4 * D
ALPHA = (2.0 * DEPTH) ** 0.25
EPS = 1e-5
GLA_HEADS, GLA_K, GLA_V, GLA_RANK = 4, 256, 512, 16
HG_PAIRS = 8
GATE_NORM = 16.0
LB_LEAST = 2.0 ** -60
NLEVEL = 9
RING = 8
SPLIT = 4
AHEAD = 3
ADA_W = 1024


class Stage:

    def __init__(self, before, iters, steps, ada=None, emptied_by=""):
        self.before, self.iters, self.steps = before, iters, steps
        self.emptied_by = emptied_by
        self.emptied0 = {e: before.emptied0[e] + before.iters * before.emptied_by.count(e) if before else 0 for e in "AV"}
        self.ada = ada or {}
        self.n_ada = sum(self.ada.values())
        order = [("w", g) for g in range(min(AHEAD, steps))]
        a = 0
        for s in range(max(steps, 1)):
            for _ in range(self.ada.get(s, 0)):
                order.append(("a", a))
                a += 1
            if s + AHEAD < steps:
                order.append(("w", s + AHEAD))
        self.order = order
        self.place = {item: pos for pos, item in enumerate(order)}
        self.per = len(order)
        self.w0 = before.w0 + before.iters * before.steps if before else 0
        self.p0 = before.p0 + before.iters * len(before.emptied_by) if before else 0
        self.a0 = before.a0 + before.iters * before.n_ada if before else 0
        self.r0 = before.r0 + before.iters * before.per if before else 0
        assert iters == 1 or (self.per % RING == 0 and steps % SPLIT == 0)

    def tile(self, n, g):
        return self.w0 + n * self.steps + g

    def emptied(self, n, p):
        e = self.emptied_by[p]
        return e, self.emptied0[e] + n * self.emptied_by.count(e) + self.emptied_by[:p + 1].count(e)

    def bank(self, p):
        return 2 * ((self.p0 + p) % 2)

    def bank_free(self, n, p):
        if p >= 2:
            return self.emptied(n, p - 2)
        st, p = self, p - 2
        if not isinstance(n, int) or n > 0:
            return self.emptied(n - 1, p + len(self.emptied_by))
        while p < 0:
            st = st.before
            if st is None or not st.emptied_by:
                return None
            p += len(st.emptied_by) * st.iters
        return st.emptied(p // len(st.emptied_by), p % len(st.emptied_by))

    def split_slot(self, g):
        return (self.w0 + g) % SPLIT

    def ring(self, n, kind, i):
        if kind == "w" and i >= self.steps:
            pos = self.per + i - self.steps
        else:
            pos = self.place[(kind, i)]
        if isinstance(n, int):
            r = self.r0 + n * self.per + pos
            return r % RING, r // RING + 1
        return (self.r0 + pos) % RING, (self.r0 + pos) // RING + 1 + n * (self.per // RING)

    def evicted(self, n, pos):
        st, n, pos = self, n, pos - RING
        while pos < 0:
            if isinstance(n, int) and n == 0:
                st = st.before
                if st is None:
                    return None
                n, pos = st.iters - 1, pos + st.per
            else:
                n, pos = n - 1, pos + st.per
        kind, i = st.order[pos]
        return kind, (st.w0 + n * st.steps if kind == "w" else st.a0 + n * st.n_ada) + i


ADA0 = Stage(None, 4, 0, {0: KB})
HG = Stage(ADA0, HG_PAIRS, 16, {3: 3, 4: 3, 5: 3, 6: 3, 7: 4}, "AVAV")
HGO = Stage(HG, 1, 32, emptied_by="V" * 8)
MLP0 = Stage(HGO, 4, 64, {s: 1 for s in range(48)}, "A" * 8 + "V" * 8)
LOW = Stage(MLP0, 1, 4, emptied_by="A")
GLA = Stage(LOW, GLA_HEADS, 24, emptied_by="AAAAVV")
GLO = Stage(GLA, 1, 32, emptied_by="V" * 8)
MLP1 = Stage(GLO, 4, 64, emptied_by="A" * 8 + "V" * 8)
OUT_ORDER = [(0, 0), (0, 1), (0, 2), (1, 0), (1, 1), (1, 2), (0, 3), (1, 3)] + [
    (p, t) for p in range(2, 8) for t in range(4)]
OUT_DONE = [6, 7] + [4 * p + 3 for p in range(2, 8)]


class Memory:

    def __init__(self, nc):
        self.nc = nc
        self.at = (nc.sbuf_base + 31) // 32 * 32
        self.top = nc.sbuf_usable_end

    def put(self, name, shape, dtype=F32, at=None):
        size = int(np.prod(shape[1:])) * (1 if dtype == U8 else 4)
        size = (size + 31) // 32 * 32
        start = self.at if at is None else at
        assert start + size <= self.top, (name, start + size - self.top)
        t = self.nc.alloc_sbuf_tensor_at(name, list(shape), dtype, offset=start)
        if at is None:
            self.at = start + size
        return t

    def scratch(self, regions, items):
        out, spots = {}, [list(r) for r in regions]
        sized = [(int(np.prod(i[1][1:])) * (1 if U8 in i else 4), i) for i in items]
        for size, (name, shape, *dtype) in sorted(sized, key=lambda si: -si[0]):
            size = (size + 31) // 32 * 32
            spot = min((s for s in spots if s[0] + size <= s[1]), key=lambda s: s[1] - s[0], default=None)
            assert spot, (name, size, [b - a for a, b in spots])
            out[name.split(".")[1]] = self.put(name.replace(".", "_"), shape, dtype[0] if dtype else F32, at=spot[0])
            spot[0] += size
        return out


def build_program(nc, A):
    mem = Memory(nc)
    raw = mem.put("raw", [P, RING, 1024])
    w_hi = mem.put("w_hi", [P, SPLIT, 4, 256], F32R)
    w_lo = mem.put("w_lo", [P, SPLIT, 4, 256], F32R)
    a_hi = mem.put("a_hi", [P, KB, T], F32R)
    a_lo = mem.put("a_lo", [P, KB, T], F32R)
    z = mem.put("z", [P, KB, T])
    mod_at = mem.at
    mod = mem.put("mod", [P, DEPTH, 6 * KB, NSEQ])
    ident = mem.put("ident", [P, P])
    ones = mem.put("ones", [P, P])
    masks = mem.put("masks", [P, 8, P], U8)
    bmask = mem.put("bmask", [P, NB])
    b_ada_at = mem.at
    b_ada = mem.put("b_ada_t", [P, DEPTH, 6 * KB])
    lnv = mem.put("lnv", [P, 2, DEPTH, 2, KB])
    vec = mem.put("vec", [P, 56])
    lbv = mem.put("lbv", [P, 4, KB])
    eps = mem.put("eps", [P, 1])
    c_t_at = mem.at
    c_t = mem.put("c_t", [P, KB, 32])
    c1 = mem.put("c1", [P, KB, NSEQ])
    c0 = mem.put("c0", [P, KB, NSEQ])
    awb = mem.put("awb", [P, 2, KB])
    mu = mem.put("mu", [P, T])
    rstd_at = mem.at
    rstd = mem.put("rstd", [P, T])
    act0 = mem.at
    act_hi = mem.put("act_hi", [P, KB, T], F32R)
    act_lo = mem.put("act_lo", [P, KB, T], F32R)
    half, act1, end = act0 + KB * T * 4, mem.at, mem.top

    o_buf = mem.put("o_buf", [P, KB, T], at=act0)
    boot = mem.scratch([(act0, act1), (act1, end)], [
        ("boot.x", [P, 3, D]), ("boot.c", [P, D]), ("boot.rows", [P, 4, P]),
        ("boot.masks", [P, 8, P]), ("boot.c_f", [P, KB, NSEQ]),
        ("boot.c_e", [P, KB, NSEQ]), ("boot.ada", [P, 256])])
    ln = mem.scratch([(act0, act1)], [("ln.sq", [P, KB, T]), ("ln.h", [P, 2, 4, T])])
    mlp_b = mem.scratch([(act1, end)], [("mlp.r", [P, 2, 2, T]), ("mlp.ada", [P, 768]), ("mlp.zs", [P, 2, TS])])
    common = lambda m: [(f"{m}.x", [P, 2, 2, T]), (f"{m}.q", [P, 2, T]), (f"{m}.k", [P, 2, T]),
                        (f"{m}.pre", [P, 2, T]), (f"{m}.suf", [P, 2, T]), (f"{m}.qd", [P, 2, TS]),
                        (f"{m}.dec", [P, 2, NB])]
    hg = mem.scratch([(half, act1), (act1, end)], common("hg") + [
        ("hg.v", [P, 2, T]), ("hg.g", [P, 2, T]), ("hg.att", [P, 2, 3, P]), ("hg.atts", [64, 2, TS]),
        ("hg.tm", [P, 2, 4, P]), ("hg.ts", [96, 4, P], F32R), ("hg.vsm", [96, 2, NB, P], F32R), ("hg.sq", [P, T]),
        ("hg.s0", [P, 2, NB, P]), ("hg.sp", [P, 2, P]), ("hg.ada", [P, 256])])
    gl = mem.scratch([(mod_at, mod_at + 6 * KB * NSEQ * 4), (c_t_at, rstd_at),
                      (b_ada_at, b_ada_at + DEPTH * 6 * KB * 4), (half, act1), (act1, end)],
                     [("gl.sp", [P, GLA_V]), ("gl.low", [P, T])] + common("gl") + [
        ("gl.v", [P, 4, T]), ("gl.g", [P, 4, T]), ("gl.att", [P, 3, P]), ("gl.atts", [64, TS]),
        ("gl.vt", [P, 2, GLA_V]), ("gl.kt", [P, 2, 2, P]), ("gl.vs", [96, GLA_V], F32R), ("gl.ks", [96, 2, P], F32R),
        ("gl.ksm", [96, 2, 2, P], F32R), ("gl.s0", [P, 4, 2, GLA_V]), ("gl.s1", [P, 2, 2, GLA_V]), ("gl.gk2", [P, 2, P])])
    yout = mem.scratch([(act0, act1)], [("yout.y", [P, 3, D])])["y"]

    main = nc.alloc_psum_tensor("main", [P, 4, 512], F32)
    b4, b5, b6, b7 = (nc.alloc_psum_tensor(f"bank{i}", [P, 512], F32) for i in (4, 5, 6, 7))

    sems = {}

    def S(name):
        if name not in sems:
            sems[name] = nc.alloc_semaphore(name)
        return sems[name]

    raw_loaded = [S(f"raw_loaded{i}") for i in range(RING)]
    hi_ready = S("hi_ready")
    lo_ready = S("lo_ready")
    tile_done = S("tile_done")
    ada_used = S("ada_used")
    panel_read = {"A": S("panel_read_act"), "V": S("panel_read_dve")}
    act_step, dve_step, pool_step = S("act_step"), S("dve_step"), S("pool_step")
    ada_copied = S("ada_copied")
    ada_turned = S("ada_turned")
    mod_ready = S("mod_ready")
    boot_loaded, boot_set = S("boot_loaded"), S("boot_set")
    boot_turned, boot_read = S("boot_turned"), S("boot_read")
    c_exp, c_ready, lb_exp, lb_ready, lb_logs = S("c_exp"), S("c_ready"), S("lb_exp"), S("lb_ready"), S("lb_logs")
    a_float = S("a_float")
    a_sample = S("a_sample")
    a_high = S("a_high")
    a_ready = S("a_ready")
    act_high, act_ready = S("act_high"), S("act_ready")
    z_done = S("z_done")
    z_ready = S("z_ready")
    ln_sum, ln_mean, ln_centered = S("ln_sum"), S("ln_mean"), S("ln_centered")
    ln_parts, ln_parts_out = S("ln_parts"), S("ln_parts_out")
    ln_squared, ln_var, ln_rstd, ln_scaled = S("ln_squared"), S("ln_var"), S("ln_rstd"), S("ln_scaled")
    y_turned, y_read, y_stored = S("y_turned"), S("y_read"), S("y_stored")
    y_ready = S("y_ready")
    h_terms = S("h_terms")
    z_before = {HGO: 0, MLP0: 8, GLO: 8 + 8 * MLP0.iters, MLP1: 16 + 8 * MLP0.iters}
    act_base = {2: 0, 5: 8 * MLP0.iters}

    def mixer(m, loads, stores):
        names = ("gate_log gate_lin gate_mix gate_soft gates_ready k_ready silu_soft silu_lin silu_exp exp_ready sums_ready "
                 "level_ready level_done level_read kd_exp kd_ready turned turned_read s_turned "
                 "s_turned_read s_split s_masked o_done o_read oi_done oi_read squared summed rstd_ready o_ready "
                 "att_set ps_done ps_read ps_stored ss_done ss_read gk_done gk_read gk2_loaded gk2_set").split()
        return {name: S(f"{m}_{name}") for name in names} | {
            "s0_loaded": [S(f"{m}_s0_loaded{i}") for i in range(loads)],
            "s_stored": [S(f"{m}_s_stored{i}") for i in range(stores)]}

    H, G = mixer("hg", 2, 2), mixer("gl", 4, 2)

    w_ada, w_up, w_down = A["w_ada"], A["w_up"], A["w_down"]
    hg_in, hg_out, gla_in, gla_out = A["hg_w_in"][0], A["hg_w_out"][0], A["gla_w_in"][0], A["gla_w_out"][0]

    def cols(start, size=256):
        return slice(start, start + size) if isinstance(start, int) else bass.ds(start, size)

    def weights(w, row, col):
        return w[cols(row, 512), :].rearrange("(k p) n -> p k n", p=P)[:, :, cols(col)]

    def halves(t, L, second):
        m = 1 << (L - 1)
        if L <= 2:
            v = t.rearrange("p h t -> p (h t)").rearrange("p (b c) -> p b c", c=2 * m)
            return v[:, :, m:] if second else v[:, :, :m]
        v = t[:, :, 0:TP].rearrange("p h (b c) -> p h b c", c=2 * m)
        return v[:, :, :, m:] if second else v[:, :, :, :m]

    def last_of(v):
        m = v.shape[-1]
        v = v[:, :, m - 1:m] if len(v.shape) == 3 else v[:, :, :, m - 1:m]
        return v.to_broadcast([*v.shape[:-1], m])

    def sample_last(t):
        return t[:, :, TP:T].rearrange("p h (b t) -> p h b t", t=TB)[:, :, :, TB - 1]

    def level_mask(L, n):
        return masks[:, L, :].unsqueeze(1).to_broadcast([P, n, P])

    def seqs(v):
        return v.rearrange("p k (b t) -> p k b t", t=TB)

    def per_token(v):
        return v.unsqueeze(3).to_broadcast([P, v.shape[1], NB, TB])

    def per_seq(v):
        return v.unsqueeze(2).to_broadcast([P, v.shape[1], NSEQ])

    def panel(st, p, n=2):
        return main[:, st.bank(p):st.bank(p) + n, 0:T]

    hg_state = A["state_hgrn"][0].rearrange("b h k v -> h k b v")
    hg_state_out = A["new_hgrn_sample"][0].rearrange("b h k v -> h k b v")
    gl_state = A["state_gla"][0].rearrange("b h (j k) v -> h b k j v", j=2)
    gl_state_out = A["new_gla_sample"][0].rearrange("b h (j k) v -> h b k j v", j=2)

    def in_register(engine, *values):
        for value in values:
            if not isinstance(value, int):
                engine.compute_val(value)

    def mixer_stored(engine, M, per_slot, prompt):
        for stored in M["s_stored"]:
            engine.wait_ge(stored, 16 * per_slot)
        engine.wait_ge(M["ps_stored"], 16 * prompt)

    def mixer_stores(engine, i):
        if i == 0:
            mixer_stored(engine, H, HG_PAIRS, HG_PAIRS)
        elif i == 2:
            mixer_stored(engine, G, GLA_HEADS * NB // 2, GLA_HEADS * 2)

    block = nc.Block()
    block.__enter__()

    @block.sync
    def _(sp):
        rows = boot["rows"]
        boots = [
            (ident[:, :], A["const_ident"]), (boot["masks"][:, :, :], A["const_masks"]), (bmask[:, :], A["const_bmask"]),
            (rows[0:96, 0, :], A["b_ada"][0].rearrange("(r c) -> r c", c=P)),
            (rows[0:96, 1, :], A["b_ada"][1].rearrange("(r c) -> r c", c=P)),
            (rows[0:64, 2, :], A["ln_w"].rearrange("l i (r c) -> (l i r) c", c=P)),
            (rows[64:128, 2, :], A["ln_b"].rearrange("l i (r c) -> (l i r) c", c=P)),
            (rows[0:16, 3, :], A["hg_lb_raw"][0].rearrange("(r c) -> r c", c=P)),
            (rows[16:32, 3, :], A["hg_norm_w"][0].rearrange("(r c) -> r c", c=P)),
            (rows[32:48, 3, :], A["gla_norm_w"][0].rearrange("(r c) -> r c", c=P)),
            (rows[48:56, 3, :], A["gla_b_gk"][0].rearrange("(r c) -> r c", c=P)),
            (boot["c"][0:1, :], A["c_prompt"]), (boot["c"][1:NSEQ, :], A["c_sample"]),
            (boot["x"][:, 0, :], A["x_prompt"][0, 0:P, :]), (boot["x"][:, 1, :], A["x_prompt"][0, P:TP, :]),
            (boot["x"][0:TS, 2, :], A["x_sample"].rearrange("b t d -> (b t) d")),
        ]
        assert len(boots) == BOOT_LOADS
        for dst, src in boots:
            sp.dma_start(dst, src).then_inc(boot_loaded, 16)

        def load(st, n, source):
            for pos, (kind, i) in enumerate(st.order):
                slot, _ = st.ring(n, kind, i)
                before = st.evicted(n, pos)
                if before:
                    in_register(sp, before[1] + 1)
                    if not isinstance(n, int):
                        sp.wait_ge(boot_loaded, 16)
                    sp.wait_ge(lo_ready if before[0] == "w" else ada_used, before[1] + 1)
                dst = raw[:, slot, :]
                if kind == "w":
                    dst = dst.rearrange("p (k n) -> p k n", k=4)
                sp.dma_start(dst, source(n, kind, i)).then_inc(raw_loaded[slot], 16)

        def run(st, source):
            load(st, 0, source)
            if st.iters > 1:
                with sp.Fori(1, st.iters) as n:
                    load(st, n, source)

        def ada_tile(layer, kb, col):
            return w_ada[layer, kb * P:(kb + 1) * P, cols(col, ADA_W)]

        def hg_tile(n, kind, i):
            if kind == "a":
                return ada_tile(0, i, n * ADA_W + 2 * D)
            return weights(hg_in, i % 4 * 512, n * 256 + (D, 0, 2 * D, 3 * D)[i // 4])

        def mlp_tile(layer):
            def source(n, kind, i):
                if kind == "a":
                    return ada_tile(1, i // 3, n * 3 * ADA_W + i % 3 * ADA_W)
                if i < 32:
                    return weights(w_up[layer], i % 4 * 512, n * D + i // 4 * 256)
                return weights(w_down[layer], n * D + i % 4 * 512, (i // 4 - 8) * 256)
            return source

        def gla_tile(n, kind, i):
            start = (n * 256, n * 256 + GLA_HEADS * GLA_K, n * 512 + D, n * 512 + D + 256,
                     n * 512 + 2 * D, n * 512 + 2 * D + 256)[i // 4]
            return weights(gla_in, i % 4 * 512, start)

        def out_tile(w):
            return lambda n, kind, i: weights(w, OUT_ORDER[i][1] * 512, OUT_ORDER[i][0] * 256)

        run(ADA0, lambda n, kind, i: ada_tile(0, i, n * ADA_W))
        run(HG, hg_tile)
        run(HGO, out_tile(hg_out))
        run(MLP0, mlp_tile(0))
        run(LOW, lambda n, kind, i: weights(gla_in, i * 512, gla_in.shape[1] - 256))
        run(GLA, gla_tile)
        run(GLO, out_tile(gla_out))
        run(MLP1, mlp_tile(1))
        mixer_stored(sp, H, HG_PAIRS, HG_PAIRS)
        mixer_stored(sp, G, GLA_HEADS * NB // 2, GLA_HEADS * 2)
        sp.wait_ge(y_stored, 16 * 12)

    @block.tensor
    def _(pe):
        mm, turn = nc.tensor.matmul, nc.tensor.transpose

        def gemm(st, n, g, p, t, x_hi, x_lo, blocks=(0, 1), between=None):
            if t == 0:
                free = st.bank_free(n, p)
                if free:
                    pe.wait_ge(panel_read[free[0]], free[1])
            pe.wait_ge(lo_ready, st.tile(n, g) + 1)
            slot = st.split_slot(g)
            for k in range(4):
                kb = 4 * t + k
                if k == 2 and between:
                    between()
                for j in blocks:
                    out = main[:, st.bank(p) + j, 0:T]
                    hi, lo = (w[:, slot, k, j * P:(j + 1) * P] for w in (w_hi, w_lo))
                    mm(out, hi, x_hi[:, kb, :], start=kb == 0, stop=False)
                    mm(out, hi, x_lo[:, kb, :], start=False, stop=False)
                    last = mm(out, lo, x_hi[:, kb, :], start=False, stop=kb == KB - 1)
            last.then_inc(tile_done, 1)

        def ada(st, n, i, kb, bank, col, first):
            slot, count = st.ring(n, "a", i)
            pe.wait_ge(raw_loaded[slot], 16 * count)
            for j in range(4):
                last = mm(bank[32 * j:32 * j + 32, col:col + 256], c_t[:, kb, :], raw[:, slot, j * 256:(j + 1) * 256],
                          start=first, stop=kb == KB - 1, skip_group_check=True, tile_position=(0, 32 * j))
            last.then_inc(ada_used, 1)

        def ada_turn(count, places, src):
            pe.wait_ge(ada_copied, count)
            for i, place in enumerate(places):
                last = turn(place, src[:, i * P:(i + 1) * P], ident[:, :])
            last.then_inc(ada_turned, 1)

        pe.wait_ge(boot_loaded, 16 * BOOT_LOADS)
        pe.wait_ge(boot_set, 1)
        groups = 0

        def turn_samples(bank, at, src, copies=3):
            for j in range(copies):
                last = mm(bank[32 * j:32 * j + 32, at:at + P], src, ident[:, :], start=True, stop=True,
                          skip_group_check=True, tile_position=(0, 32 * j))
            return last

        def sample_scores(at, lhs, rhs, start=True, stop=True):
            for j in range(2):
                mm(b6[32 * j:32 * j + 32, at:at + 32], lhs, rhs, start=start, stop=stop, skip_group_check=True,
                   tile_position=(0, 32 * j))

        def turn_group(parts):
            nonlocal groups
            if groups >= 4:
                pe.wait_ge(boot_read, groups - 3)
            for at, src, r in parts:
                last = turn(main[:, groups % 4, at:at + r], src, ident[0:r, 0:r])
            last.then_inc(boot_turned, 1)
            groups += 1

        rows = boot["rows"]
        turn_group([(0, rows[0:96, 0, :], 96), (96, rows[0:96, 1, :], 96)])
        turn_group([(0, rows[:, 2, :], P), (P, rows[0:56, 3, :], 56)])
        turn_group([(NSEQ * kb, boot["c"][0:NSEQ, kb * P:(kb + 1) * P], NSEQ) for kb in range(KB)])
        for i in range(3):
            r = P if i < 2 else TS
            for c in range(4):
                turn_group([(r * j, boot["x"][0:r, i, (4 * c + j) * P:(4 * c + j + 1) * P], r) for j in range(4)])
        pe.wait_ge(c_ready, 1)
        for n in range(4):
            if n:
                pe.wait_ge(ada_copied, n)
            for i in range(KB):
                ada(ADA0, n, i, i, b5, 0, i == 0)
            if n:
                pe.wait_ge(mod_ready, n)
            ada_turn(n + 1, [b7[:, 0:P], b7[:, P:2 * P]], boot["ada"])

        def hg_level(n, L, prev):
            x = hg["x"][:, L % 2]
            lhs, rhs = (hg["k"], hg["q"]) if L == 0 else (x, x)
            bank = b4 if L % 2 == 0 else b5
            if L == 0:
                pe.wait_ge(panel_read["V"], HG.emptied(n, 1)[1])
                pe.wait_ge(H["k_ready"], n + 1)
                if prev:
                    pe.wait_ge(H["ss_read"], 4 * n - 3)
                    pe.wait_ge(H["rstd_ready"], 2 * n)
            else:
                pe.wait_ge(H["level_ready"], 8 * n + L)
            if L == 1:
                pe.wait_ge(ada_copied, 5 + n)
                if prev:
                    pe.wait_ge(H["ss_read"], 4 * n - 1)
            if L >= 1:
                pe.wait_ge(H["level_read"], 9 * n + (L if L <= 2 else L - 1))
            if L <= 2:
                for h in range(2):
                    sample_scores(64 * L + 32 * h, lhs[:, h, TP:T], rhs[:, h, TP:T])
            for h in range(2):
                if L == 8:
                    last = mm(bank[:, h * P:(h + 1) * P], x[:, h, 0:P], x[:, h, P:TP], start=True, stop=True)
                else:
                    for t in range(2):
                        c = slice(t * P, (t + 1) * P)
                        last = mm(bank[:, (2 * h + t) * P:(2 * h + t + 1) * P], lhs[:, h, c], rhs[:, h, c],
                                  start=True, stop=True)
            last.then_inc(H["level_done"], 1)

        def hg_turn(pn, h):
            if h == 0:
                pe.wait_ge(H["kd_ready"], pn + 1)
                pe.wait_ge(panel_read["A"], HG.emptied(pn, 2)[1])
                pe.wait_ge(H["level_read"], 9 * pn + 3)
            else:
                pe.wait_ge(H["turned_read"], 2 * pn + 1)
            for j, (src, t) in enumerate([("v", 0), ("v", 1), ("k", 0), ("k", 1)]):
                src = hg["v"] if src == "v" else hg["x"][:, 1]
                last = turn(b6[:, j * P:(j + 1) * P], src[:, h, t * P:(t + 1) * P], ident[:, :])
            last.then_inc(H["turned"], 1)

        def hg_sample_turn(pn):
            pe.wait_ge(mod_ready, 5 + pn)
            for j, (src, h) in enumerate([("v", 0), ("v", 1), ("k", 0), ("k", 1)]):
                src = hg["v"] if src == "v" else hg["x"][:, 1]
                last = turn_samples(b7, j * P, src[:, h, TP:T])
            last.then_inc(H["s_turned"], 1)

        def hg_out_head(pn, h):
            pe.wait_ge(H["turned_read"], 2 * pn + h + 1)
            pe.wait_ge(H["s_split"], pn + 1)
            pe.wait_ge(H["level_read"], 9 * pn + 9)
            pe.wait_ge(H["s0_loaded"][h], 16 * (pn + 1))
            if h == 1:
                pe.wait_ge(H["o_read"], 2 * pn + 1)
            tm, att, s0, qd = hg["tm"], hg["att"], hg["s0"], hg["qd"]
            mm(b7[:, 0:TP], tm[:, h, 0, :], att[:, h, 0:2, :].rearrange("p a t -> p (a t)"), start=True, stop=False,
               skip_group_check=True)
            mm(b7[:, P:TP], tm[:, h, 1, :], att[:, h, 2, :], start=False, stop=False, skip_group_check=True)
            mm(b7[:, TP:T], hg["ts"][0:64, h, :].bitcast(F32), hg["atts"][:, h, :], start=False, stop=False,
               skip_group_check=True)
            for b in range(NB):
                last = mm(b7[:, TP + TB * b:TP + TB * (b + 1)], s0[:, h, b, :], qd[:, h, TB * b:TB * (b + 1)],
                          start=False, stop=b == NB - 1, skip_group_check=True)
            last.then_inc(H["o_done"], 1)

        def hg_sum(pn, h):
            pe.wait_ge(H["o_read"], 2 * pn + h + 1)
            if h == 0:
                pe.wait_ge(H["turned_read"], 2 * pn + 2)
            else:
                pe.wait_ge(H["rstd_ready"], 2 * pn + 1)
            mm(b6[:, 0:T], ones[:, :], hg["sq"][:, :], start=True, stop=True).then_inc(H["summed"], 1)

        def hg_prompt_state(pn):
            pe.wait_ge(H["turned_read"], 2 * pn + 2)
            for h in range(2):
                for t in range(2):
                    last = mm(b4[:, h * P:(h + 1) * P], hg["tm"][:, h, 2 + t, :], hg["tm"][:, h, t, :],
                              start=t == 0, stop=t == 1)
            last.then_inc(H["ps_done"], 1)

        def hg_sample_state(pn, x, ada_count):
            h, half_ = divmod(x, 2)
            pe.wait_ge(H["s_masked"], 2 * pn + h + 1)
            if x == 0:
                pe.wait_ge(H["ps_read"], pn + 1)
            elif x == 1:
                pe.wait_ge(H["o_read"], 2 * pn + 2)
            elif x == 2:
                pe.wait_ge(ada_copied, ada_count)
            else:
                pe.wait_ge(H["ss_read"], 4 * pn + 2)
            mm((b4, b7, b5, b7)[x][:, :], hg["ts"][:, 2 + h, :],
               hg["vsm"][:, h, 4 * half_:4 * half_ + 4, :].rearrange("p b v -> p (b v)"), start=True, stop=True
               ).then_inc(H["ss_done"], 1)

        def hg_step(n, s, own, prev):
            pn = n - 1
            if prev:
                if s == 0:
                    hg_level(pn, 6, False)
                elif s == 1:
                    hg_level(pn, 7, False)
                elif s == 2:
                    hg_level(pn, 8, False)
                elif s == 3:
                    hg_turn(pn, 0)
                    hg_sample_turn(pn)
                elif s == 4:
                    hg_turn(pn, 1)
                elif s == 5:
                    hg_out_head(pn, 0)
                elif s == 6:
                    hg_sum(pn, 0)
                    hg_prompt_state(pn)
                elif s == 7:
                    hg_out_head(pn, 1)
                elif s == 8:
                    hg_sum(pn, 1)
                if 8 <= s <= 11:
                    hg_sample_state(pn, s - 8, 5 + n if own else 4 + n)
            if own:
                if s in HG.ada:
                    first = sum(c for t, c in HG.ada.items() if t < s)
                    if first == 0 and prev:
                        pe.wait_ge(H["level_read"], 9 * n - 1)
                    for i in range(first, first + HG.ada[s]):
                        ada(HG, n, i, i, b5, 0, i == 0)
                if s >= 10:
                    hg_level(n, s - 10, prev)
                if s == 12:
                    if prev:
                        pe.wait_ge(H["ss_read"], 4 * n)
                    ada_turn(5 + n, [b7[:, 0:P], b7[:, P:2 * P]], hg["ada"])

        def hg_iteration(n, prev):
            for s in range(16):
                if s < 4 and isinstance(n, int):
                    pe.wait_ge(a_ready, s + 1)
                gemm(HG, n, s, s // 4, s % 4, a_hi, a_lo, between=lambda: hg_step(n, s, True, prev))

        def out_projection(st, tail, event):
            for s, (p, t) in enumerate(OUT_ORDER):
                if s < 6:
                    tail(2 * s)
                if s < 3 or s == 6:
                    pe.wait_ge(a_ready, 4 * event + t + 1)
                gemm(st, 0, s, p, t, a_hi, a_lo, between=lambda: [
                    tail(x) for x in ((2 * s + 1,) if s < 5 else (11, 12) if s == 5 else ())])

        def layer_norm(i, event):
            pe.wait_ge(ln_sum, i + 1)
            mm(b4[:, 0:T], ones[:, :], mu[:, :], start=True, stop=True).then_inc(ln_mean, 1)
            for c in range(4):
                pe.wait_ge(ln_squared, 4 * i + c + 1)
                for j in range(4):
                    last = mm(b5[32 * j:32 * j + 32, 0:T], ones[:, 0:32], ln["sq"][:, 4 * c + j, :], start=c == 0,
                              stop=c == 3, skip_group_check=True, tile_position=(0, 32 * j))
            last.then_inc(ln_parts, 1)
            pe.wait_ge(ln_parts_out, i + 1)
            mm(b4[:, 0:T], ones[:, :], rstd[:, :], start=True, stop=True).then_inc(ln_var, 1)

        def mlp(st, event, with_ada):
            with pe.Fori(0, st.iters) as n:
                for s in range(64):
                    if s < 4:
                        pe.wait_ge(a_ready, 4 * event + s + 1)
                    if 32 <= s < 36:
                        for kp in (1, 2):
                            pe.wait_ge(act_ready, act_base[event] + 8 * n + 2 * (s - 32) + kp)
                    up = s < 32
                    gemm(st, n, s, s // 4, s % 4, *((a_hi, a_lo) if up else (act_hi, act_lo)))
                    if with_ada and s in st.ada:
                        kb, c = divmod(s, 3)
                        if s == 0:
                            pe.wait_ge(mod_ready, 12 + n)
                        ada(st, n, s, kb, (b4, b4, b5)[c], (0, 256, 0)[c], kb == 0 and c != 1)
                    if with_ada and s == 52:
                        ada_turn(13 + n, [b6[:, i * P:(i + 1) * P] for i in range(4)] +
                                 [b7[:, i * P:(i + 1) * P] for i in range(2)], mlp_b["ada"])

        hg_iteration(0, False)
        with pe.Fori(1, HG_PAIRS) as n:
            hg_iteration(n, True)
        out_projection(HGO, lambda s: hg_step(HG_PAIRS, s, False, True), 1)
        layer_norm(0, 2)
        mlp(MLP0, 2, True)
        layer_norm(1, 3)

        def gl_level(n, L, prev):
            x = gl["x"][:, L % 2]
            lhs, rhs = (gl["k"], gl["q"]) if L == 0 else (x, x)
            bank = b4 if L % 2 == 0 else b5
            if L == 0:
                pe.wait_ge(panel_read["A"], GLA.emptied(n, 1)[1])
                if prev:
                    pe.wait_ge(G["ss_read"], 8 * n)
                    pe.wait_ge(G["o_read"], 4 * n)
            else:
                pe.wait_ge(G["level_ready"], 8 * n + L)
            if L == 1 and prev:
                pe.wait_ge(G["rstd_ready"], n)
            if L >= 1:
                pe.wait_ge(G["level_read"], 9 * n + (L if L <= 2 else L - 1))
            if L <= 2:
                for j in range(2):
                    sample_scores(32 * L, lhs[:, j, TP:T], rhs[:, j, TP:T], j == 0, j == 1)
            tiles = [(slice(0, P), slice(P, TP))] if L == 8 else [(slice(t * P, (t + 1) * P),) * 2 for t in range(2)]
            for t, (rows_, cols_) in enumerate(tiles):
                for j in range(2):
                    last = mm(bank[:, t * P:(t + 1) * P], lhs[:, j, rows_], rhs[:, j, cols_], start=j == 0, stop=j == 1)
            last.then_inc(G["level_done"], 1)

        def gl_gate(n, j, prev):
            if j == 0:
                if prev:
                    pe.wait_ge(G["ps_read"], 2 * n)
                else:
                    pe.wait_ge(panel_read["A"], LOW.emptied(0, 0)[1])
                pe.wait_ge(G["gk2_loaded"], 16 * (n + 1))
            else:
                pe.wait_ge(G["gk_read"], 2 * n + 1)
            mm(b6[:, 0:T], gl["gk2"][:, j, :], gl["low"][:, :],
               start=True, stop=True).then_inc(G["gk_done"], 1)

        def gl_turn_v(n, t):
            if t == 0:
                pe.wait_ge(panel_read["A"], GLA.emptied(n, 3)[1])
                pe.wait_ge(G["level_read"], 9 * n + 3)
            bank = (b6, b7)[t]
            for j in range(4):
                last = turn(bank[:, j * P:(j + 1) * P], gl["v"][:, j, t * P:(t + 1) * P], ident[:, :])
            last.then_inc(G["turned"], 1)

        def gl_turn_vs(n):
            pe.wait_ge(G["turned_read"], 3 * n + 1)
            for j in range(4):
                last = turn_samples(b6, j * P, gl["v"][:, j, TP:T])
            last.then_inc(G["s_turned"], 1)

        def gl_turn_k(n):
            pe.wait_ge(G["kd_ready"], n + 1)
            pe.wait_ge(G["level_read"], 9 * n + 8)
            for t in range(2):
                for j in range(2):
                    last = turn(b5[:, (2 * t + j) * P:(2 * t + j + 1) * P], gl["x"][:, 1, j, t * P:(t + 1) * P],
                                ident[:, :])
            last.then_inc(G["turned"], 1)
            pe.wait_ge(G["turned_read"], 3 * n + 2)
            for j in range(2):
                last = turn_samples(b7, j * P, gl["x"][:, 1, j, TP:T])
            last.then_inc(G["s_turned"], 1)

        def gl_prompt_state(n, j):
            if j == 0:
                pe.wait_ge(G["turned_read"], 3 * n + 3)
                pe.wait_ge(G["s_split"], 2 * n + 1)
            else:
                pe.wait_ge(G["ps_read"], 2 * n + 1)
            for t in range(2):
                last = mm(b6[:, :], gl["kt"][:, t, j, :], gl["vt"][:, t, :], start=t == 0, stop=t == 1)
            last.then_inc(G["ps_done"], 1)

        def gl_intra(n):
            pe.wait_ge(G["s_split"], 2 * n + 2)
            pe.wait_ge(G["level_read"], 9 * n + 3)
            for v in range(4):
                mm(b7[:, 32 * v:32 * v + 32], gl["vs"][0:64, v * P:(v + 1) * P].bitcast(F32), gl["atts"][:, :], start=v == 0,
                   stop=False, skip_group_check=True)

        def gl_sample(n, b):
            slot = b % 4
            pe.wait_ge(G["s0_loaded"][slot], 32 * n + 16 * (b // 4 + 1))
            pe.wait_ge(G["s_masked"], 8 * n + b + 1)
            if b == 0:
                pe.wait_ge(G["level_read"], 9 * n + 9)
                pe.wait_ge(G["turned_read"], 3 * n + 3)
            else:
                pe.wait_ge(G["ss_read"], 8 * n + b)
            for v in range(4):
                for j in range(2):
                    last = mm(b7[:, 32 * v + TB * b:32 * v + TB * (b + 1)], gl["s0"][:, slot, j, v * P:(v + 1) * P],
                              gl["qd"][:, j, TB * b:TB * (b + 1)], start=False, stop=j == 1 and b == NB - 1,
                              skip_group_check=True)
            if b == NB - 1:
                last.then_inc(G["oi_done"], 1)
            for j, bank in enumerate((b4, b5)):
                last = mm(bank[:, :], gl["ksm"][:, b % 2, j, :], gl["vs"][:, :], start=True, stop=True)
            last.then_inc(G["ss_done"], 1)

        def gl_out_block(n, v):
            bank = (b6, b7)[v % 2]
            if v == 1:
                pe.wait_ge(G["oi_read"], n + 1)
            if v >= 2:
                pe.wait_ge(G["o_read"], 4 * n + v - 1)
            mm(bank[:, 0:TP], gl["vt"][:, 0, v * P:(v + 1) * P], gl["att"][:, 0:2, :].rearrange("p a t -> p (a t)"),
               start=True, stop=False, skip_group_check=True)
            mm(bank[:, P:TP], gl["vt"][:, 1, v * P:(v + 1) * P], gl["att"][:, 2, :], start=False, stop=True,
               skip_group_check=True).then_inc(G["o_done"], 1)

        def gl_sum(n):
            pe.wait_ge(G["squared"], n + 1)
            pe.wait_ge(G["ss_read"], 8 * n + 8)
            for v in range(4):
                last = mm(b5[:, 0:T], ones[:, :], gl["v"][:, v, :], start=v == 0, stop=v == 3)
            last.then_inc(G["summed"], 1)

        def gl_step(n, s, own, prev):
            pn = n - 1
            if prev:
                if s <= 6:
                    gl_sample(pn, s + 1)
                if s == 0:
                    gl_prompt_state(pn, 1)
                if s == 6:
                    pe.wait_ge(*((G["gk_read"], 2 * n + 2) if own else (G["ps_read"], 2 * pn + 2)))
                if 6 <= s <= 9:
                    gl_out_block(pn, s - 6)
                if s == 10:
                    gl_sum(pn)
            if own:
                if s == 2:
                    gl_gate(n, 0, prev)
                elif s == 4:
                    gl_gate(n, 1, prev)
                elif 11 <= s <= 19:
                    gl_level(n, s - 11, prev)
                if s == 17:
                    gl_turn_v(n, 0)
                    gl_turn_v(n, 1)
                elif s == 19:
                    gl_turn_vs(n)
                elif s == 20:
                    gl_turn_k(n)
                elif s == 22:
                    gl_prompt_state(n, 0)
                elif s == 23:
                    gl_intra(n)
                    gl_sample(n, 0)

        for s in range(4):
            pe.wait_ge(a_ready, 4 * 3 + s + 1)
            gemm(LOW, 0, s, 0, s, a_hi, a_lo, blocks=(1,))

        def gl_iteration(n, prev):
            for s in range(24):
                gemm(GLA, n, s, s // 4, s % 4, a_hi, a_lo, between=lambda: gl_step(n, s, True, prev))

        gl_iteration(0, False)
        with pe.Fori(1, GLA_HEADS) as n:
            gl_iteration(n, True)
        out_projection(GLO, lambda s: gl_step(GLA_HEADS, s, False, True), 4)
        layer_norm(2, 5)
        mlp(MLP1, 5, False)
        layer_norm(3, None)

        for c in range(4):
            pe.wait_ge(y_ready, c + 1)
            for i in range(3):
                g = 3 * c + i
                r = P if i < 2 else TS
                if g >= 4:
                    pe.wait_ge(y_read, g - 3)
                for j in range(4):
                    last = turn(main[0:r, g % 4, j * P:(j + 1) * P], z[:, 4 * c + j, i * P:i * P + r], ident[:, :])
                last.then_inc(y_turned, 1)

    @block.scalar
    def _(act):
        tally = Tally(act, act_step)
        step = tally.step
        F = nc.scalar.activation

        def cast(st, n, g):
            slot, count = st.ring(n, "w", g)
            act.wait_ge(raw_loaded[slot], 16 * count)
            if not isinstance(n, int) or st.tile(n, g) >= SPLIT:
                act.wait_ge(tile_done, st.tile(n, g) - (SPLIT - 1))
            F(w_hi[:, st.split_slot(g)].rearrange("p k n -> p (k n)"), raw[:, slot, :], ACT.Copy).then_inc(hi_ready, 1)

        def panel_done(st, n, g):
            act.wait_ge(tile_done, st.tile(n, g) + 1)

        def split_h(e, first, src_sem=None, src_base=0):
            for c in range(4):
                if src_sem is not None:
                    act.wait_ge(src_sem, src_base + c + 1)
                if c >= 2:
                    act.wait_ge(a_ready, 4 * e + c - 1)
                for i in range(4):
                    kb = 4 * c + i
                    last = F(ln["h"][:, c % 2, i, 0:TP], z[:, kb, 0:TP], ACT.Identity, scale=c1[:, kb, 0:1],
                             bias=c0[:, kb, 0:1])
                last.then_inc(a_float, 1)
                act.wait_ge(a_float, 4 * first + c + 1)
                act.wait_ge(a_sample, 4 * first + c + 1)
                F(a_hi[:, 4 * c:4 * c + 4, :], ln["h"][:, c % 2], ACT.Copy).then_inc(a_high, 1)

        def split_o(c):
            F(a_hi[:, 4 * c:4 * c + 4, :], o_buf[:, 4 * c:4 * c + 4, :], ACT.Copy).then_inc(a_high, 1)

        nc.scalar.preload_act_table_set("natural_log_exp_and_others")
        act.wait_ge(boot_set, 1)
        act.wait_ge(boot_read, 3)
        F(boot["c_e"][:, :, :], boot["c_f"][:, :, :], ACT.Exp, scale=-1.0).then_inc(c_exp, 1)
        act.wait_ge(lb_ready, 1)
        F(lbv[:, 0, :], lbv[:, 0, :], ACT.Exp).then_inc(lb_exp, 1)
        act.wait_ge(lb_ready, 2)
        F(lbv[:, 1, :], lbv[:, 0, :], ACT.Ln, scale=-1.0, bias=ones[:, 0:1])
        F(lbv[:, 2, :], lbv[:, 3, :], ACT.Ln).then_inc(lb_logs, 1)
        for n in range(4):
            act.wait_ge(ada_used, KB * (n + 1))
            if n:
                act.wait_ge(ada_turned, n)
            F(boot["ada"][:, :], b5[:, 0:256], ACT.Copy).then_inc(ada_copied, 1)
        act.wait_ge(boot_turned, 15)
        for g in range(AHEAD):
            cast(HG, 0, g)
        act.wait_ge(h_terms, 1)
        split_h(0, 0)

        def silu_soft(M, x, src):
            step(F(x, src, ACT.Abs))
            step(F(x, x, ACT.Exp, scale=-1.0))
            F(x, x, ACT.Ln, bias=ones[:, 0:1]).then_inc(M["silu_soft"], 1)

        def silu_exp(M, count, x):
            act.wait_ge(M["silu_lin"], count)
            F(x, x, ACT.Exp).then_inc(M["silu_exp"], 1)

        def level_exp(M, buf, n, L):
            if L == 1:
                act.wait_ge(M["gates_ready"], n + 1)
            else:
                act.wait_ge(M["sums_ready"], 8 * n + L - 1)
            if L >= 3:
                act.wait_ge(M["level_done"], 9 * n + L - 1)
            x = buf["x"][:, L % 2]
            F(halves(x, L, False), halves(buf["suf"], L, False), ACT.Exp)
            F(halves(x, L, True), halves(buf["pre"], L, True), ACT.Exp).then_inc(M["exp_ready"], 1)

        def key_exp(M, buf, n):
            act.wait_ge(M["sums_ready"], 8 * n + 8)
            act.wait_ge(M["level_done"], 9 * n + 8)
            F(buf["x"][:, 1], buf["suf"][:, :, :], ACT.Exp)
            F(buf["qd"][:, :, :], buf["pre"][:, :, TP:T], ACT.Exp)
            F(buf["dec"][:, :, :], sample_last(buf["pre"]), ACT.Exp).then_inc(M["kd_exp"], 1)

        def gate_soft(M, buf, n):
            t1, t2 = buf["x"][:, 0], buf["x"][:, 1]
            step(F(t2, t1, ACT.Abs))
            step(F(t2, t2, ACT.Exp, scale=-1.0))
            F(t2, t2, ACT.Ln, bias=ones[:, 0:1]).then_inc(M["gate_log"], 1)

        def head_rstd(M, wait, src, width):
            act.wait_ge(M["summed"], wait)
            step(F(rstd[:, :], src[:, 0:T], ACT.Ln, scale=1.0 / width, bias=eps[:, :]))
            F(rstd[:, :], rstd[:, :], ACT.Exp, scale=-0.5).then_inc(M["rstd_ready"], 1)

        def hg_pair(pn):
            return cols(2 * pn, 2)

        def hg_load(n, h):
            act.dma_start(hg["s0"][:, h], hg_state[cols(2 * n + h, 1)].rearrange("h k b v -> (h k) b v")
                          ).then_inc(H["s0_loaded"][h], 16)

        def hg_step(n, s, own, prev):
            pn = n - 1
            if prev:
                if s == 0:
                    silu_exp(H, 2 * pn + 2, hg["g"][:, :, :])
                if s in (0, 1):
                    level_exp(H, hg, pn, s + 7)
                elif s == 2:
                    key_exp(H, hg, pn)
                elif s in (3, 4):
                    h = s - 3
                    act.wait_ge(H["turned"], 2 * pn + h + 1)
                    F(hg["tm"][:, h].rearrange("p a c -> p (a c)"), b6[:, :], ACT.Copy).then_inc(H["turned_read"], 1)
                    if h == 0:
                        act.wait_ge(H["s_turned"], pn + 1)
                        F(hg["ts"].rearrange("p a c -> p (a c)"), b7[0:96, :], ACT.Copy).then_inc(H["s_turned_read"], 1)
                elif s in (5, 7):
                    h = (s - 5) // 2
                    act.wait_ge(H["o_done"], 2 * pn + h + 1)
                    if h == 1:
                        act.wait_ge(H["summed"], 2 * pn + 1)
                    F(o_buf[:, cols(2 * pn + h, 1), :].rearrange("p a t -> p (a t)"), b7[:, 0:T], ACT.Copy)
                    F(hg["sq"][:, :], b7[:, 0:T], ACT.Square).then_inc(H["o_read"], 1)
                elif s in (6, 8):
                    h = (s - 6) // 2
                    if h == 1:
                        act.wait_ge(H["o_ready"], 2 * pn + 1)
                    head_rstd(H, 2 * pn + h + 1, b6, P)
                if s == 7:
                    act.wait_ge(H["ps_done"], pn + 1)
                    F(hg["sp"].rearrange("p h v -> p (h v)"), b4[:, 0:256], ACT.Copy).then_inc(H["ps_read"], 1)
                    act.wait_ge(H["ps_read"], pn + 1)
                    act.dma_start(A["new_hgrn_prompt"][0, 0].rearrange("h k v -> k h v")[:, hg_pair(pn), :],
                                  hg["sp"][:, :, :]).then_inc(H["ps_stored"], 16)
                if s in (10, 12):
                    h = (s - 10) // 2
                    act.wait_ge(H["ss_read"], 4 * pn + 2 * h + 2)
                    act.dma_start(hg_state_out[cols(2 * pn + h, 1)].rearrange("h k b v -> (h k) b v"),
                                  hg["s0"][:, h]).then_inc(H["s_stored"][h], 16)
                if s == 12:
                    act.wait_ge(H["ps_stored"], 16 * (pn + 1))
                if s == 14 and own:
                    for h in range(2):
                        act.wait_ge(H["s_stored"][h], 16 * (pn + 1))
                        hg_load(n, h)
            if own:
                if s == 5:
                    if prev:
                        act.wait_ge(H["s_turned"], pn + 1)
                    panel_done(HG, n, 3)
                    t1, t2 = hg["x"][:, 0], hg["x"][:, 1]
                    F(t1, panel(HG, 0), ACT.Copy).then_inc(panel_read["A"], 1)
                    act.wait_ge(panel_read["A"], HG.emptied(n, 0)[1])
                    gate_soft(H, hg, n)
                elif s == 6:
                    t1 = hg["x"][:, 0]
                    act.wait_ge(H["gate_lin"], n + 1)
                    for h in range(2):
                        last = F(hg["k"][:, h], t1[:, h], ACT.Exp, bias=lbv[:, 1, cols(2 * n + h, 1)])
                    last.then_inc(H["k_ready"], 1)
                    act.wait_ge(H["gate_mix"], n + 1)
                    step(F(hg["suf"][:, :, :], hg["suf"][:, :, :], ACT.Exp))
                    F(hg["suf"][:, :, :], hg["suf"][:, :, :], ACT.Ln, bias=ones[:, 0:1]).then_inc(H["gate_soft"], 1)
                elif s == 8:
                    act.wait_ge(ada_used, HG.a0 + KB * (n + 1))
                    if not isinstance(n, int) or n:
                        act.wait_ge(ada_turned, 4 + n)
                    F(hg["ada"][:, :], b5[:, 0:256], ACT.Copy).then_inc(ada_copied, 1)
                    panel_done(HG, n, 7)
                    silu_soft(H, hg["q"][:, :, :], panel(HG, 1))
                elif s == 9:
                    silu_exp(H, 2 * n + 1, hg["q"][:, :, :])
                elif s == 12:
                    panel_done(HG, n, 11)
                    F(hg["v"][:, :, :], panel(HG, 2), ACT.Copy).then_inc(panel_read["A"], 1)
                if s >= 10:
                    level_exp(H, hg, n, s - 9)

        def hg_iteration(n, prev):
            for s in range(16):
                cast(HG, n, s + AHEAD)
                hg_step(n, s, True, prev)
            panel_done(HG, n, 15)
            if prev:
                act.wait_ge(H["o_ready"], 2 * n)
            silu_soft(H, hg["g"][:, :, :], panel(HG, 3))

        act.wait_ge(a_ready, 4)
        for h in range(2):
            hg_load(0, h)
        hg_iteration(0, False)
        tally.start("hg_act")
        with act.Fori(1, HG_PAIRS) as n:
            tally.at(n, 1)
            hg_iteration(n, True)
        tally.end(HG_PAIRS - 1)

        def out_projection(st, tail):
            act.wait_ge(tile_done, st.w0)
            for c in range(3):
                split_o(c)
            for s in range(32):
                cast(st, 0, s + AHEAD)
                for x in ((2 * s, 2 * s + 1) if s < 5 else (10, 11, 12, 13) if s == 5 else ()):
                    tail(x)
                if s == 5:
                    (act.wait_ge(H["o_ready"], 16) if st is HGO else act.wait_ge(G["o_ready"], GLA_HEADS))
                    split_o(3)

        def out_first(st):
            act.wait_ge(*((H["o_ready"], 14) if st is HGO else (G["o_ready"], GLA_HEADS - 1)))

        out_first(HGO)
        out_projection(HGO, lambda s: hg_step(HG_PAIRS, s, False, True))

        def layer_norm(i, e):
            mixer_stores(act, i)
            for c in range(4):
                act.wait_ge(ln_centered, 4 * i + c + 1)
                F(ln["sq"][:, 4 * c:4 * c + 4, :], z[:, 4 * c:4 * c + 4, :], ACT.Square).then_inc(ln_squared, 1)
            act.wait_ge(ln_parts, i + 1)
            F(rstd[:, :], b5[:, 0:T], ACT.Copy).then_inc(ln_parts_out, 1)
            act.wait_ge(ln_var, i + 1)
            step(F(rstd[:, :], b4[:, 0:T], ACT.Ln, scale=1.0 / (32 * D), bias=eps[:, :]))
            F(rstd[:, :], rstd[:, :], ACT.Exp, scale=-0.5).then_inc(ln_rstd, 1)
            if e is not None:
                split_h(e, i + 1, ln_scaled, 4 * i)

        def mlp(st, e, n, with_ada, last_n=False):
            for s in range(64):
                if not (last_n and s + AHEAD >= 64):
                    cast(st, n, s + AHEAD)
                if s % 4 == 0 and 4 <= s <= 32:
                    p = s // 4 - 1
                    panel_done(st, n, s - 1)
                    r = mlp_b["r"][:, p % 2]
                    if p >= 2:
                        act.wait_ge(act_ready, act_base[e] + 8 * n + p - 1)
                    F(r, panel(st, p), ACT.Relu).then_inc(panel_read["A"], 1)
                    act.wait_ge(panel_read["A"], st.emptied(n, p)[1])
                    F(act_hi[:, 2 * p:2 * p + 2, :], r, ACT.Square).then_inc(act_high, 1)
                if with_ada and s == 49:
                    act.wait_ge(ada_used, st.a0 + 48 * (n + 1))
                    act.wait_ge(ada_turned, 12 + n)
                    F(mlp_b["ada"][:, 0:512], b4[:, :], ACT.Copy)
                    F(mlp_b["ada"][:, 512:768], b5[:, 0:256], ACT.Copy).then_inc(ada_copied, 1)

        layer_norm(0, 2)
        with act.Fori(0, MLP0.iters) as n:
            mlp(MLP0, 2, n, True)
        layer_norm(1, 3)

        def gl_load(n, b):
            act.dma_start(gl["s0"][:, b % 4], gl_state[cols(n, 1), b].rearrange("h k j v -> (h k) j v")
                          ).then_inc(G["s0_loaded"][b % 4], 16)

        def gl_store(n, b):
            act.wait_ge(G["ss_read"], 8 * n + b + 1)
            act.dma_start(gl_state_out[cols(n, 1), b].rearrange("h k j v -> (h k) j v"), gl["s1"][:, b % 2]
                          ).then_inc(G["s_stored"][b % 2], 16)

        def gl_state_copy(n, j):
            act.wait_ge(G["ps_done"], 2 * n + j + 1)
            F(gl["sp"][:, :], b6[:, :], ACT.Copy).then_inc(G["ps_read"], 1)
            act.wait_ge(G["ps_read"], 2 * n + j + 1)
            act.dma_start(A["new_gla_prompt"][0, 0].rearrange("h (j k) v -> h k j v", j=2)[cols(n, 1), :, j, :]
                          .rearrange("h k v -> (h k) v"), gl["sp"][:, :]).then_inc(G["ps_stored"], 16)

        def gl_step(n, s, own, prev):
            pn = n - 1
            if prev:
                if s == 1:
                    act.wait_ge(G["ps_stored"], 16 * (2 * pn + 1))
                    gl_state_copy(pn, 1)
                if s == 0:
                    silu_exp(G, 2 * pn + 2, gl["g"][:, 2:4, :])
                if s <= 7:
                    gl_store(pn, s)
                    if s < 4 or own:
                        gl_load(*((pn, s + 4) if s < 4 else (n, s - 4)))
                if s == 6:
                    act.wait_ge(G["oi_done"], pn + 1)
                    F(o_buf[:, cols(4 * pn, 4), TP:T], b7[:, 0:128].rearrange("p (v t) -> p v t", v=4), ACT.Copy
                      ).then_inc(G["oi_read"], 1)
                for v, at in enumerate((6, 7, 8, 9)):
                    if s == at:
                        act.wait_ge(G["o_done"], 4 * pn + v + 1)
                        F(o_buf[:, cols(4 * pn + v, 1), 0:TP].rearrange("p a t -> p (a t)"), (b6, b7)[v % 2][:, 0:TP],
                          ACT.Copy).then_inc(G["o_read"], 1)
                if s == 9:
                    act.wait_ge(G["att_set"], 1)
                    act.wait_ge(G["o_read"], 4 * pn + 4)
                    F(gl["v"][:, :, :], o_buf[:, cols(4 * pn, 4), :], ACT.Square).then_inc(G["squared"], 1)
                if s == 10:
                    head_rstd(G, pn + 1, b5, GLA_V)
            if own:
                if s == 0:
                    if prev:
                        act.wait_ge(G["gk_done"], 2 * n)
                    act.dma_start(gl["gk2"][P - GLA_RANK:P], A["gla_w_gk2"][0].rearrange("r (a c) -> r a c", c=P)
                                  [:, cols(2 * n, 2), :]).then_inc(G["gk2_loaded"], 16)
                if s in (2, 4):
                    j = (s - 2) // 2
                    act.wait_ge(G["gk_done"], 2 * n + j + 1)
                    F(gl["x"][:, 0, j], b6[:, 0:T], ACT.Identity, bias=vec[:, cols(48 + 2 * n + j, 1)]
                      ).then_inc(G["gk_read"], 1)
                if s == 5:
                    act.wait_ge(G["gk_read"], 2 * n + 2)
                    gate_soft(G, gl, n)
                    panel_done(GLA, n, 3)
                    F(gl["q"][:, :, :], panel(GLA, 0), ACT.Copy, scale=GLA_K ** -0.5).then_inc(panel_read["A"], 1)
                elif s == 8:
                    panel_done(GLA, n, 7)
                    F(gl["k"][:, :, :], panel(GLA, 1), ACT.Copy).then_inc(panel_read["A"], 1)
                elif s in (12, 16):
                    j = (s - 12) // 4
                    panel_done(GLA, n, s - 1)
                    F(gl["v"][:, 2 * j:2 * j + 2, :], panel(GLA, 2 + j), ACT.Copy).then_inc(panel_read["A"], 1)
                elif s == 20:
                    panel_done(GLA, n, 19)
                    silu_soft(G, gl["g"][:, 0:2, :], panel(GLA, 4))
                elif s == 21:
                    silu_exp(G, 2 * n + 1, gl["g"][:, 0:2, :])
                if 11 <= s <= 18:
                    level_exp(G, gl, n, s - 10)
                if s == 18:
                    for t in range(2):
                        act.wait_ge(G["turned"], 3 * n + t + 1)
                        F(gl["vt"][:, t, :], (b6, b7)[t][:, :], ACT.Copy).then_inc(G["turned_read"], 1)
                elif s == 19:
                    key_exp(G, gl, n)
                elif s == 20:
                    act.wait_ge(G["s_turned"], 2 * n + 1)
                    F(gl["vs"][:, :], b6[0:96, :], ACT.Copy).then_inc(G["s_turned_read"], 1)
                elif s == 21:
                    act.wait_ge(G["turned"], 3 * n + 3)
                    F(gl["kt"].rearrange("p t j c -> p (t j c)"), b5[:, :], ACT.Copy).then_inc(G["turned_read"], 1)
                    act.wait_ge(G["s_turned"], 2 * n + 2)
                    F(gl["ks"].rearrange("p j c -> p (j c)"), b7[0:96, 0:256], ACT.Copy).then_inc(G["s_turned_read"], 1)
                elif s == 23:
                    if prev:
                        act.wait_ge(G["ps_stored"], 32 * n)
                    gl_state_copy(n, 0)

        def gl_iteration(n, prev):
            for s in range(24):
                cast(GLA, n, s + AHEAD)
                gl_step(n, s, True, prev)
            panel_done(GLA, n, 23)
            silu_soft(G, gl["g"][:, 2:4, :], panel(GLA, 5))

        act.wait_ge(G["gk2_set"], 1)
        for b in range(4):
            gl_load(0, b)
        for s in range(4):
            cast(LOW, 0, s + AHEAD)
        panel_done(LOW, 0, 3)
        F(gl["low"][:, :], main[:, LOW.bank(0) + 1, 0:T], ACT.Copy).then_inc(panel_read["A"], 1)
        gl_iteration(0, False)
        tally.start("gl_act")
        with act.Fori(1, GLA_HEADS) as n:
            tally.at(n, 1)
            gl_iteration(n, True)
        tally.end(GLA_HEADS - 1)
        out_first(GLO)
        out_projection(GLO, lambda s: gl_step(GLA_HEADS, s, False, True))
        layer_norm(2, 5)
        with act.Fori(0, MLP1.iters - 1) as n:
            mlp(MLP1, 5, n, False)
        mlp(MLP1, 5, MLP1.iters - 1, False, last_n=True)
        layer_norm(3, None)
        for c in range(4):
            act.wait_ge(ln_scaled, 4 * 3 + c + 1)
            for kb in range(4 * c, 4 * c + 4):
                last = F(z[:, kb, :], z[:, kb, :], ACT.Identity, scale=lnv[:, 0, 1, 1, kb:kb + 1],
                         bias=lnv[:, 1, 1, 1, kb:kb + 1])
            last.then_inc(y_ready, 1)
        ys = A["y_prompt"][0, 0:P, :], A["y_prompt"][0, P:TP, :], A["y_sample"].rearrange("b t d -> (b t) d")
        for c in range(4):
            for i in range(3):
                r = P if i < 2 else TS
                act.wait_ge(y_read, 3 * c + i + 1)
                act.dma_start(ys[i][:, c * 512:(c + 1) * 512], yout[0:r, i, c * 512:(c + 1) * 512]).then_inc(y_stored, 16)

    @block.vector
    def _(dve):
        tally = Tally(dve, dve_step)
        step = tally.step
        V = nc.vector

        def split(st, n, g):
            slot, _ = st.ring(n, "w", g)
            dve.wait_ge(hi_ready, st.tile(n, g) + 1)
            s = st.split_slot(g)
            V.tensor_tensor(w_lo[:, s].rearrange("p k n -> p (k n)"), raw[:, slot, :],
                            w_hi[:, s].rearrange("p k n -> p (k n)").bitcast(F32), ALU.subtract).then_inc(lo_ready, 1)

        def low_part(e, c, src):
            dve.wait_ge(a_high, 4 * e + c + 1)
            V.tensor_tensor(a_lo[:, 4 * c:4 * c + 4, :], src, a_hi[:, 4 * c:4 * c + 4, :].bitcast(F32),
                            ALU.subtract).then_inc(a_ready, 1)

        def sample_h(c):
            k = slice(4 * c, 4 * c + 4)
            h = seqs(ln["h"][:, c % 2, :, TP:T])
            step(V.tensor_tensor(h, seqs(z[:, k, TP:T]), per_token(c1[:, k, 1:NSEQ]), ALU.mult))
            V.tensor_tensor(h, h, per_token(c0[:, k, 1:NSEQ]), ALU.add).then_inc(a_sample, 1)

        def mod_update(layer, block0, groups, count, src):
            dve.wait_ge(ada_turned, count)
            for i in range(groups):
                out = mod[:, layer, cols(block0 + 8 * i, 8), :].rearrange("p (j s) q -> p s j q", s=2)
                bias = b_ada[:, layer, cols(block0 + 8 * i, 8)].rearrange("p (j s) -> p s j", s=2)
                for s_ in range(2):
                    ps = src[i][:, s_ * P:(s_ + 1) * P].rearrange("p (j q) -> p j q", q=32)[:, :, 0:NSEQ]
                    last = V.tensor_tensor(out[:, s_], ps, bias[:, s_].unsqueeze(2).to_broadcast([P, 4, NSEQ]), ALU.add)
            last.then_inc(mod_ready, 1)

        dve.wait_ge(boot_loaded, 16 * BOOT_LOADS)
        step(V.memset(c_t[:, :, :], 0.0))
        step(V.tensor_copy(masks[:, :, :], boot["masks"][:, :, :]))
        dve.wait_ge(boot_turned, 1)
        for layer in range(2):
            last = V.tensor_copy(b_ada[:, layer, :], main[:, 0, 96 * layer:96 * layer + 96])
        last.then_inc(boot_read, 1)
        dve.wait_ge(boot_read, 1)
        V.tensor_scalar(b_ada[:, :, KB:3 * KB], b_ada[:, :, KB:3 * KB], 1.0, None, ALU.add)
        step(V.tensor_scalar(b_ada[:, :, 4 * KB:6 * KB], b_ada[:, :, 4 * KB:6 * KB], 1.0, None, ALU.add))
        dve.wait_ge(boot_turned, 2)
        V.tensor_copy(lnv.rearrange("p a l i k -> p (a l i k)"), main[:, 1, 0:P])
        V.tensor_copy(vec[:, :], main[:, 1, P:P + 56]).then_inc(boot_read, 1)
        dve.wait_ge(boot_turned, 3)
        V.tensor_copy(boot["c_f"].rearrange("p k q -> p (k q)"), main[:, 2, 0:KB * NSEQ]).then_inc(boot_read, 1)
        dve.wait_ge(c_exp, 1)
        ce = boot["c_e"][:, :, :]
        step(V.tensor_scalar(ce, ce, 1.0, None, ALU.add))
        step(V.reciprocal(ce, ce))
        V.tensor_tensor(c_t[:, :, 0:NSEQ], boot["c_f"][:, :, :], ce, ALU.mult).then_inc(c_ready, 1)
        step(V.tensor_tensor(lbv[:, 1, :], vec[:, 0:KB], vec[:, 0:KB], ALU.max))
        V.tensor_tensor(lbv[:, 0, :], vec[:, 0:KB], lbv[:, 1, :], ALU.subtract).then_inc(lb_ready, 1)
        dve.wait_ge(lb_exp, 1)
        step(V.reciprocal(lbv[:, 1, :], lbv[:, 0, :]))
        step(V.tensor_tensor(lbv[:, 0, :], lbv[:, 0, :], lbv[:, 1, :], ALU.mult))
        step(V.tensor_tensor(lbv[:, 1, :], lbv[:, 0, :], lbv[:, 0, :], ALU.subtract))
        step(V.tensor_scalar(lbv[:, 0, :], lbv[:, 1, :], 0.0, 1.0 - 1e-6, ALU.max, ALU.min))
        V.tensor_scalar(lbv[:, 3, :], lbv[:, 0, :], LB_LEAST, None, ALU.max).then_inc(lb_ready, 1)
        dve.wait_ge(lb_logs, 1)
        step(V.tensor_scalar(lbv[:, 3, :], lbv[:, 0, :], LB_LEAST, -1e30, ALU.is_lt, ALU.mult))
        step(V.tensor_tensor(lbv[:, 2, :], lbv[:, 2, :], lbv[:, 3, :], ALU.add))
        for i in range(3):
            r = P if i < 2 else TS
            for c in range(4):
                g = 3 + 4 * i + c
                dve.wait_ge(boot_turned, g + 1)
                V.tensor_scalar(z[:, 4 * c:4 * c + 4, i * P:i * P + r],
                                main[:, g % 4, 0:4 * r].rearrange("p (k t) -> p k t", k=4), ALPHA, None, ALU.mult
                                ).then_inc(boot_read, 1)
        for n in range(4):
            mod_update(0, 8 * n, 1, n + 1, [b7])
        dve.wait_ge(mod_ready, 4)
        V.tensor_scalar(c1[:, :, :], mod[:, 0, KB:2 * KB, :], 1.0 / ALPHA, None, ALU.mult)
        V.tensor_copy(c0[:, :, :], mod[:, 0, 0:KB, :]).then_inc(h_terms, 1)
        for g in range(AHEAD):
            split(HG, 0, g)
        dve.wait_ge(h_terms, 1)
        for c in range(4):
            if c >= 2:
                dve.wait_ge(a_ready, c - 1)
            sample_h(c)
            low_part(0, c, ln["h"][:, c % 2])
        dve.wait_ge(a_ready, 4)
        V.memset(hg["att"][:, :, :, :], 0.0).then_inc(H["att_set"], 1)
        V.memset(hg["atts"][:, :, :], 0.0).then_inc(H["att_set"], 1)

        def silu_lin(M, count, x, src):
            dve.wait_ge(M["silu_soft"], count)
            V.scalar_tensor_tensor(out=x, in0=src, scalar=0.0, in1=x, op0=ALU.min, op1=ALU.subtract
                                   ).then_inc(M["silu_lin"], 1)

        def silu_mul(M, count, x, src, st, n, p):
            dve.wait_ge(M["silu_exp"], count)
            V.tensor_tensor(x, x, src, ALU.mult).then_inc(panel_read["V"], 1)
            dve.wait_ge(panel_read["V"], st.emptied(n, p)[1])

        def level_mul(M, buf, n, L):
            dve.wait_ge(M["exp_ready"], 8 * n + L)
            x = buf["x"][:, L % 2]
            for second, src in ((False, buf["k"]), (True, buf["q"])):
                xs = halves(x, L, second)
                last = V.tensor_tensor(xs, xs, halves(src, L, second), ALU.mult)
            last.then_inc(M["level_ready"], 1)

        def hg_read(n, L, prev):
            if L == 0 and prev:
                dve.wait_ge(H["o_done"], 2 * n)
            in_register(dve, 9 * n + L, 9 * n + L + 1)
            dve.wait_ge(H["att_set"], 2)
            if L:
                dve.wait_ge(H["level_read"], 9 * n + L)
            dve.wait_ge(H["level_done"], 9 * n + L + 1)
            bank = b4 if L % 2 == 0 else b5
            if L <= 2:
                for q in (0, 32):
                    mask = masks[q:q + 32, L, q:q + 32].unsqueeze(1).to_broadcast([32, 2, 32])
                    V.copy_predicated(hg["atts"][q:q + 32, :, :], mask,
                                      b6[q:q + 32, 64 * L:64 * L + 64].rearrange("p (h t) -> p h t", h=2))
            if L == 8:
                V.tensor_copy(hg["att"][:, :, 1, :], bank[:, 0:256].rearrange("p (h t) -> p h t", h=2)
                              ).then_inc(H["level_read"], 1)
            else:
                for h in range(2):
                    last = V.copy_predicated(hg["att"][:, h, 0:3:2, :], level_mask(L, 2),
                                             bank[:, 256 * h:256 * h + 256].rearrange("p (a t) -> p a t", a=2))
                last.then_inc(H["level_read"], 1)

        def sample_split(M, count, parts):
            dve.wait_ge(M["s_turned_read"], count)
            for part, src in parts:
                last = V.tensor_tensor(part, src, part.bitcast(F32), ALU.subtract)
            last.then_inc(M["s_split"], 1)

        def key_mul(M, buf, n):
            dve.wait_ge(M["kd_exp"], n + 1)
            V.tensor_tensor(buf["x"][:, 1], buf["x"][:, 1], buf["k"][:, :, :], ALU.mult)
            V.tensor_tensor(buf["qd"][:, :, :], buf["qd"][:, :, :], buf["q"][:, :, TP:T], ALU.mult
                            ).then_inc(M["kd_ready"], 1)

        def hg_step(n, s, own, prev):
            pn = n - 1
            if prev:
                if s == 0:
                    silu_mul(H, 2 * pn + 2, hg["g"][:, :, :], panel(HG, 3), HG, pn, 3)
                if s in (0, 1):
                    level_mul(H, hg, pn, s + 7)
                if s <= 2:
                    hg_read(pn, s + 6, True)
                if s == 2:
                    key_mul(H, hg, pn)
                if s == 4:
                    sample_split(H, pn + 1, [
                        (hg["ts"][32:64, 0:2, :].rearrange("p a c -> p (a c)"), b7[32:64, 0:256]),
                        (hg["ts"][64:96, 2:4, :].rearrange("p a c -> p (a c)"), b7[64:96, 256:512])])
                if s == 5:
                    dve.wait_ge(H["s_split"], pn + 1)
                    for h in range(2):
                        V.tensor_tensor(hg["vsm"][:, h],
                                        hg["ts"][:, h, :].bitcast(F32).unsqueeze(1).to_broadcast([96, NB, P]),
                                        bmask[0:96, :].unsqueeze(2).to_broadcast([96, NB, P]), ALU.mult
                                        ).then_inc(H["s_masked"], 1)
                for x, at in enumerate((8, 9, 10, 11)):
                    if s == at:
                        h = x // 2
                        dve.wait_ge(H["ss_done"], 4 * pn + x + 1)
                        for i in range(4):
                            b = 4 * (x % 2) + i
                            last = V.scalar_tensor_tensor(
                                out=hg["s0"][:, h, b, :], in0=hg["s0"][:, h, b, :], scalar=hg["dec"][:, h, b:b + 1],
                                in1=(b4, b7, b5, b7)[x][:, i * P:(i + 1) * P], op0=ALU.mult, op1=ALU.add)
                        last.then_inc(H["ss_read"], 1)
                if s in (6, 8):
                    h = (s - 6) // 2
                    dve.wait_ge(H["rstd_ready"], 2 * pn + h + 1)
                    o = o_buf[:, cols(2 * pn + h, 1), :].rearrange("p a t -> p (a t)")
                    step(V.tensor_tensor(o, o, rstd[:, :], ALU.mult))
                    V.scalar_tensor_tensor(out=o, in0=o, scalar=vec[:, cols(KB + 2 * pn + h, 1)], in1=hg["g"][:, h],
                                           op0=ALU.mult, op1=ALU.mult).then_inc(H["o_ready"], 1)
            if own:
                if s == 5:
                    t1, t2, pre, suf = hg["x"][:, 0], hg["x"][:, 1], hg["pre"], hg["suf"]
                    dve.wait_ge(H["gate_log"], n + 1)
                    step(V.scalar_tensor_tensor(out=pre[:, :, :], in0=t1, scalar=0.0, in1=t2, op0=ALU.min,
                                                op1=ALU.subtract))
                    V.tensor_tensor(t1, pre[:, :, :], t1, ALU.subtract).then_inc(H["gate_lin"], 1)
                    for h in range(2):
                        last = V.tensor_scalar(t2[:, h], pre[:, h], lbv[:, 1, cols(2 * n + h, 1)], None, ALU.add)
                    step(last)
                    for h in range(2):
                        last = V.tensor_scalar(pre[:, h], t2[:, h], lbv[:, 2, cols(2 * n + h, 1)], None, ALU.max)
                    step(last)
                    for h in range(2):
                        last = V.scalar_tensor_tensor(out=suf[:, h], in0=t2[:, h], scalar=lbv[:, 2, cols(2 * n + h, 1)],
                                                      in1=pre[:, h], op0=ALU.min, op1=ALU.subtract)
                    last.then_inc(H["gate_mix"], 1)
                elif s == 7:
                    dve.wait_ge(H["gate_soft"], n + 1)
                    step(V.tensor_tensor(hg["pre"][:, :, :], hg["pre"][:, :, :], hg["suf"][:, :, :], ALU.add))
                    V.memset(hg["suf"][:, :, :], 0.0).then_inc(H["gates_ready"], 1)
                elif s == 8:
                    silu_lin(H, 2 * n + 1, hg["q"][:, :, :], panel(HG, 1))
                elif s == 9:
                    silu_mul(H, 2 * n + 1, hg["q"][:, :, :], panel(HG, 1), HG, n, 1)
                if s >= 10:
                    level_mul(H, hg, n, s - 9)
                    hg_read(n, s - 10, prev)
                if s == 13:
                    mod_update(0, 8 * n + 2 * KB, 1, 5 + n, [b7])

        def hg_iteration(n, prev):
            for s in range(16):
                split(HG, n, s + AHEAD)
                hg_step(n, s, True, prev)
            silu_lin(H, 2 * n + 2, hg["g"][:, :, :], panel(HG, 3))

        hg_iteration(0, False)
        tally.start("hg_dve")
        with dve.Fori(1, HG_PAIRS) as n:
            tally.at(n, 1)
            hg_iteration(n, True)
        tally.end(HG_PAIRS - 1)

        def residual(st, n, p, layer, gate, j):
            src, zs = panel(st, p), mlp_b["zs"]
            for i in range(2):
                kb = 2 * j + i
                V.scalar_tensor_tensor(out=z[:, kb, 0:TP], in0=src[:, i, 0:TP], scalar=mod[:, layer, gate * KB + kb, 0:1],
                                       in1=z[:, kb, 0:TP], op0=ALU.mult, op1=ALU.add)
            k = slice(gate * KB + 2 * j, gate * KB + 2 * j + 2)
            V.tensor_tensor(seqs(zs[:, :, :]), seqs(src[:, :, TP:T]), per_token(mod[:, layer, k, 1:NSEQ]), ALU.mult
                            ).then_inc(panel_read["V"], 1)
            dve.wait_ge(panel_read["V"], st.emptied(n, p)[1])
            zk = z[:, 2 * j:2 * j + 2, TP:T]
            V.tensor_tensor(zk, zk, zs[:, :, :], ALU.add).then_inc(z_done, 1)
            dve.wait_ge(z_done, z_before[st] + 8 * n + j + 1)

        def out_projection(st, tail, e, layer):
            for c in range(3):
                low_part(e, c, o_buf[:, 4 * c:4 * c + 4, :])
            for s in range(32):
                split(st, 0, s + AHEAD)
                for x in ((2 * s, 2 * s + 1) if s < 5 else (10, 11, 12, 13) if s == 5 else ()):
                    tail(x)
                if s == 5:
                    low_part(e, 3, o_buf[:, 12:16, :])
                if s and s - 1 in OUT_DONE:
                    p = OUT_DONE.index(s - 1)
                    dve.wait_ge(tile_done, st.tile(0, s - 1) + 1)
                    if p == 0:
                        mixer_stores(dve, 2 * layer)
                        if layer:
                            dve.wait_ge(z_ready, 2)
                    residual(st, 0, p, layer, 2, p)
            dve.wait_ge(tile_done, st.tile(0, 31) + 1)
            residual(st, 0, 7, layer, 2, 7)

        out_projection(HGO, lambda s: hg_step(HG_PAIRS, s, False, True), 1, 0)

        def layer_norm(i, e):
            layer, which = divmod(i, 2)
            w, b = lnv[:, 0, layer, which, :], lnv[:, 1, layer, which, :]
            if e is not None:
                nl, shift = (i + 1) // 2, 3 * ((i + 1) % 2)
                sc = mod[:, nl, (shift + 1) * KB:(shift + 2) * KB, :]
                sh = mod[:, nl, shift * KB:(shift + 1) * KB, :]
                step(V.tensor_tensor(c1[:, :, :], sc, per_seq(w), ALU.mult))
                step(V.tensor_tensor(c0[:, :, :], sc, per_seq(b), ALU.mult))
                step(V.tensor_tensor(c0[:, :, :], c0[:, :, :], sh, ALU.add))
                V.tensor_scalar(awb[:, 0, :], w, ALPHA, None, ALU.mult)
                step(V.tensor_scalar(awb[:, 1, :], b, ALPHA, None, ALU.mult))
            dve.wait_ge(ln_mean, i + 1)
            step(V.tensor_scalar(mu[:, :], b4[:, 0:T], 1.0 / D, None, ALU.mult))
            for c in range(4):
                zc = z[:, 4 * c:4 * c + 4, :]
                V.tensor_tensor(zc, zc, mu[:, :].unsqueeze(1).to_broadcast([P, 4, T]), ALU.subtract
                                ).then_inc(ln_centered, 1)
            dve.wait_ge(ln_rstd, i + 1)

            def scale(c):
                zc = z[:, 4 * c:4 * c + 4, :]
                V.tensor_tensor(zc, zc, rstd[:, :].unsqueeze(1).to_broadcast([P, 4, T]), ALU.mult
                                ).then_inc(ln_scaled, 1)

            if e is None:
                for c in range(4):
                    scale(c)
                return
            for c in range(4):
                scale(c)
                if c >= 2:
                    dve.wait_ge(a_ready, 4 * e + c - 1)
                dve.wait_ge(ln_scaled, 4 * i + c + 1)
                sample_h(c)
                if c:
                    low_part(e, c - 1, ln["h"][:, (c - 1) % 2])
            low_part(e, 3, ln["h"][:, 1])

        def mlp(st, e, n, layer, with_ada, last_n=False):
            for s in range(64):
                if not (last_n and s + AHEAD >= 64):
                    split(st, n, s + AHEAD)
                if s % 4 == 0 and 4 <= s <= 32:
                    p = s // 4 - 1
                    r = mlp_b["r"][:, p % 2]
                    dve.wait_ge(act_high, act_base[e] + 8 * n + p + 1)
                    step(V.tensor_tensor(r, r, r, ALU.mult))
                    V.tensor_tensor(act_lo[:, 2 * p:2 * p + 2, :], r, act_hi[:, 2 * p:2 * p + 2, :].bitcast(F32),
                                    ALU.subtract).then_inc(act_ready, 1)
                if s % 4 == 0 and s > 32:
                    if s == 36:
                        dve.wait_ge(z_ready, 1 if st is MLP0 else 3)
                    dve.wait_ge(tile_done, st.tile(n, s - 1) + 1)
                    residual(st, n, s // 4 - 1, layer, 5, s // 4 - 9)
                if with_ada and s == 54:
                    mod_update(1, 24 * n, 3, 13 + n, [b6[:, 0:256], b6[:, 256:512], b7[:, 0:256]])
            dve.wait_ge(tile_done, st.tile(n, 63) + 1)
            residual(st, n, 15, layer, 5, 7)

        layer_norm(0, 2)
        tally.start("mlp0_dve")
        with dve.Fori(0, MLP0.iters) as n:
            tally.at(n, 0)
            mlp(MLP0, 2, n, 0, True)
        tally.end(MLP0.iters)
        layer_norm(1, 3)

        def gl_read(n, L, prev):
            if L == 0 and prev:
                dve.wait_ge(G["o_done"], 4 * n)
            in_register(dve, 9 * n + L, 9 * n + L + 1)
            dve.wait_ge(G["att_set"], 2)
            if L:
                dve.wait_ge(G["level_read"], 9 * n + L)
            dve.wait_ge(G["level_done"], 9 * n + L + 1)
            bank = b4 if L % 2 == 0 else b5
            if L <= 2:
                for q in (0, 32):
                    V.copy_predicated(gl["atts"][q:q + 32, :], masks[q:q + 32, L, q:q + 32],
                                      b6[q:q + 32, 32 * L:32 * L + 32])
            if L == 8:
                V.tensor_copy(gl["att"][:, 1, :], bank[:, 0:P]).then_inc(G["level_read"], 1)
            else:
                V.copy_predicated(gl["att"][:, 0:3:2, :], level_mask(L, 2),
                                  bank[:, 0:256].rearrange("p (a t) -> p a t", a=2)).then_inc(G["level_read"], 1)

        def gl_mask(n, b):
            if b >= 2:
                dve.wait_ge(G["ss_done"], 8 * n + b - 1)
            V.tensor_scalar(gl["ksm"][:, b % 2], gl["ks"][:, :, :].bitcast(F32), bmask[0:96, b:b + 1], None, ALU.mult
                            ).then_inc(G["s_masked"], 1)

        def gl_state(n, b):
            dve.wait_ge(G["ss_done"], 8 * n + b + 1)
            if b >= 2:
                dve.wait_ge(G["s_stored"][b % 2], 64 * n + 16 * (b // 2))
            for j, bank in enumerate((b4, b5)):
                last = V.scalar_tensor_tensor(out=gl["s1"][:, b % 2, j, :], in0=gl["s0"][:, b % 4, j, :],
                                              scalar=gl["dec"][:, j, b:b + 1], in1=bank[:, :],
                                              op0=ALU.mult, op1=ALU.add)
            last.then_inc(G["ss_read"], 1)

        def gl_step(n, s, own, prev):
            pn = n - 1
            if prev:
                if s == 0:
                    silu_mul(G, 2 * pn + 2, gl["g"][:, 2:4, :], panel(GLA, 5), GLA, pn, 5)
                if s <= 6:
                    gl_state(pn, s + 1)
                if s <= 5:
                    gl_mask(pn, s + 2)
                if s == 10:
                    dve.wait_ge(G["rstd_ready"], pn + 1)
                    o = o_buf[:, cols(4 * pn, 4), :]
                    step(V.tensor_tensor(o, o, rstd[:, :].unsqueeze(1).to_broadcast([P, 4, T]), ALU.mult))
                    for v in range(4):
                        o = o_buf[:, cols(4 * pn + v, 1), :].rearrange("p a t -> p (a t)")
                        last = V.scalar_tensor_tensor(out=o, in0=o, scalar=vec[:, cols(2 * KB + 4 * pn + v, 1)],
                                                      in1=gl["g"][:, v], op0=ALU.mult, op1=ALU.mult)
                    last.then_inc(G["o_ready"], 1)
            if own:
                if s == 6:
                    t1, t2, pre = gl["x"][:, 0], gl["x"][:, 1], gl["pre"][:, :, :]
                    dve.wait_ge(G["gate_log"], n + 1)
                    step(V.scalar_tensor_tensor(out=pre, in0=t1, scalar=0.0, in1=t2, op0=ALU.min, op1=ALU.subtract))
                    step(V.tensor_scalar(pre, pre, 1.0 / GATE_NORM, None, ALU.mult))
                    V.memset(gl["suf"][:, :, :], 0.0).then_inc(G["gates_ready"], 1)
                if 11 <= s <= 18:
                    level_mul(G, gl, n, s - 10)
                if 11 <= s <= 19:
                    gl_read(n, s - 11, prev)
                if s == 19:
                    key_mul(G, gl, n)
                elif s == 20:
                    silu_lin(G, 2 * n + 1, gl["g"][:, 0:2, :], panel(GLA, 4))
                elif s == 21:
                    silu_mul(G, 2 * n + 1, gl["g"][:, 0:2, :], panel(GLA, 4), GLA, n, 4)
                    sample_split(G, 2 * n + 1, [(gl["vs"][32:64, :], b6[32:64, :])])
                elif s == 22:
                    sample_split(G, 2 * n + 2, [
                        (gl["ks"][64:96].rearrange("p j c -> p (j c)"), b7[64:96, 0:256])])
                    dve.wait_ge(G["s_split"], 2 * n + 2)
                    if prev:
                        dve.wait_ge(G["ss_done"], 8 * n)
                    gl_mask(n, 0)
                    gl_mask(n, 1)
                elif s == 23:
                    if prev:
                        for stored in G["s_stored"]:
                            dve.wait_ge(stored, 64 * n)
                    gl_state(n, 0)

        def gl_iteration(n, prev):
            for s in range(24):
                split(GLA, n, s + AHEAD)
                gl_step(n, s, True, prev)
            silu_lin(G, 2 * n + 2, gl["g"][:, 2:4, :], panel(GLA, 5))

        V.memset(gl["gk2"][:, :, :], 0.0).then_inc(G["gk2_set"], 1)
        V.memset(gl["att"][:, :, :], 0.0).then_inc(G["att_set"], 1)
        V.memset(gl["atts"][:, :], 0.0).then_inc(G["att_set"], 1)
        for s in range(4):
            split(LOW, 0, s + AHEAD)
        gl_iteration(0, False)
        tally.start("gl_dve")
        with dve.Fori(1, GLA_HEADS) as n:
            tally.at(n, 1)
            gl_iteration(n, True)
        tally.end(GLA_HEADS - 1)
        out_projection(GLO, lambda s: gl_step(GLA_HEADS, s, False, True), 4, 1)
        layer_norm(2, 5)
        tally.start("mlp1_dve")
        with dve.Fori(0, MLP1.iters - 1) as n:
            tally.at(n, 0)
            mlp(MLP1, 5, n, 1, False)
        tally.end(MLP1.iters - 1)
        mlp(MLP1, 5, MLP1.iters - 1, 1, False, last_n=True)
        layer_norm(3, None)
        for g in range(12):
            c, i = divmod(g, 3)
            r = P if i < 2 else TS
            dve.wait_ge(y_turned, g + 1)
            V.tensor_copy(yout[0:r, i, c * 512:(c + 1) * 512], main[0:r, g % 4, :]).then_inc(y_read, 1)

    @block.gpsimd
    def _(pool):
        nc.gpsimd.memset(ones[:, :], 1.0)
        nc.gpsimd.memset(eps[:, :], EPS).then_inc(boot_set, 1)

        def sums(M, buf, n, steps_before):
            for L in range(1, 9):
                pool.wait_ge(M["exp_ready"], 8 * n + L)
                pre1, pre2 = (halves(buf["pre"], L, second) for second in (False, True))
                suf1 = halves(buf["suf"], L, False)
                nc.gpsimd.tensor_tensor(suf1, suf1, last_of(pre2), ALU.add).then_inc(pool_step, 1)
                pool.wait_ge(pool_step, steps_before + 8 * n + L)
                nc.gpsimd.tensor_tensor(pre2, pre2, last_of(pre1), ALU.add).then_inc(M["sums_ready"], 1)

        pool_steps = 0

        def step(instruction):
            nonlocal pool_steps
            pool_steps += 1
            instruction.then_inc(pool_step, 1)
            pool.wait_ge(pool_step, pool_steps)

        def feature_sum(i, before):
            for j in range(8):
                pool.wait_ge(z_done, before + j + 1)
                for kb in (2 * j, 2 * j + 1):
                    if kb == 0:
                        continue
                    first = z[:, 0, :] if kb == 1 else mu[:, :]
                    add = nc.gpsimd.tensor_tensor(mu[:, :], first, z[:, kb, :], ALU.add)
                    if kb < KB - 1:
                        step(add)
            add.then_inc(ln_sum, 1)

        def affine(i):
            for c in range(4):
                pool.wait_ge(a_float, 4 * (i + 1) + c + 1)
                pool.wait_ge(a_sample, 4 * (i + 1) + c + 1)
                for kb in range(4 * c, 4 * c + 4):
                    last = nc.gpsimd.tensor_scalar(z[:, kb, :], z[:, kb, :], awb[:, 0, kb:kb + 1], awb[:, 1, kb:kb + 1],
                                                   ALU.mult, ALU.add)
            last.then_inc(z_ready, 1)

        with pool.Fori(0, HG_PAIRS) as n:
            sums(H, hg, n, 0)
        pool_steps += 8 * HG_PAIRS
        feature_sum(0, z_before[HGO])
        affine(0)
        feature_sum(1, z_before[GLO] - 8)
        affine(1)
        before_gla = pool_steps
        with pool.Fori(0, GLA_HEADS) as n:
            sums(G, gl, n, before_gla)
        pool_steps += 8 * GLA_HEADS
        feature_sum(2, z_before[GLO])
        affine(2)
        feature_sum(3, z_before[MLP1] + 8 * (MLP1.iters - 1))

    block.__exit__(None, None, None)


STEPS = {"hg_act": 9, "hg_dve": 6, "gl_act": 7, "gl_dve": 3, "mlp0_dve": 8, "mlp1_dve": 8}
BOOT_LOADS = 16


class Tally:

    def __init__(self, engine, sem):
        self.engine, self.sem, self.count, self.turn = engine, sem, 0, 0

    def step(self, instruction):
        self.count += 1
        instruction.then_inc(self.sem, 1)
        self.engine.wait_ge(self.sem, self.count + self.turn)

    def start(self, name):
        self.name, self.before = name, self.count

    def at(self, n, first):
        self.turn = n * STEPS[self.name] - first * STEPS[self.name]

    def end(self, iterations):
        assert self.count - self.before == STEPS[self.name], (self.name, self.count - self.before)
        self.count, self.turn = self.before + iterations * STEPS[self.name], 0


INPUTS = ["x_prompt", "x_sample", "state_hgrn", "state_gla", "c_prompt", "c_sample", "w_ada", "b_ada", "ln_w", "ln_b",
          "hg_w_in", "hg_lb_raw", "hg_norm_w", "hg_w_out", "gla_w_in", "gla_w_gk2", "gla_b_gk", "gla_norm_w",
          "gla_w_out", "w_up", "w_down"]
OUTPUTS = [("y_prompt", (1, TP, D)), ("y_sample", (NB, TB, D)), ("new_hgrn_prompt", (1, 1, 16, P, P)),
           ("new_gla_prompt", (1, 1, GLA_HEADS, GLA_K, GLA_V)), ("new_hgrn_sample", (1, NB, 16, P, P)),
           ("new_gla_sample", (1, NB, GLA_HEADS, GLA_K, GLA_V))]


def shape_constants():
    s, t = np.arange(P)[:, None], np.arange(P)[None, :]
    masks = np.zeros((P, 8, P), np.float32)
    masks[:, 0] = s == t
    for L in range(1, 8):
        m = 1 << (L - 1)
        masks[:, L] = (s // (2 * m) == t // (2 * m)) & (s // m % 2 == 0) & (t // m % 2 == 1)
    bmask = (np.arange(P)[:, None] % TS // TB == np.arange(NB)[None, :]).astype(np.float32)
    return {"const_ident": np.eye(P, dtype=np.float32), "const_masks": masks, "const_bmask": bmask}


def kernel(**inputs):
    import concourse.bacc as _bacc
    from concourse.bass_utils import run_bass_kernel_spmd as _run

    nc = _bacc.Bacc("TRN2", target_bir_lowering=False, num_devices=1)
    arrays = {f"in_{name}": np.ascontiguousarray(inputs[name]) for name in INPUTS}
    arrays.update({f"in_{name}": a for name, a in shape_constants().items()})
    args = {}
    for name, a in arrays.items():
        args[name[3:]] = nc.dram_tensor(name, a.shape, mybir.dt.from_np(a.dtype), kind="ExternalInput").ap()
    for name, shape in OUTPUTS:
        args[name] = nc.dram_tensor(f"out_{name}", shape, F32, kind="ExternalOutput").ap()
    build_program(nc, args)
    r = _run(nc, [arrays], core_ids=[0])
    return tuple(r.results[0][f"out_{name}"] for name, _ in OUTPUTS)
```
